# Optimizing a Trainium2 kernel written in Bass

```python
import math
import jax
import jax.numpy as jnp
from jax import lax
import numpy as np

D_MODEL = 1024
BATCH = 1
SEQ = 512
DEPTH = 1
DEC_BATCH = 8
DEC_SEQ = 4
PAST_LEN = 1024
PAGE_SIZE = 128

EPS = 1e-6
NEG_INF = -1e30
FORCE_SCORE = 1e4

GDN_HEADS = 4
GDN_DK = 128
GDN_DV = 128
GDN_CONV = 4
GDN_CHUNK = 64
NSA_HEADS = 8
NSA_KV_HEADS = 2
NSA_HD = 64
NSA_GROUP = NSA_HEADS // NSA_KV_HEADS
CMP_BLOCK = 32
SEL_BLOCK = 64
SEL_TOPK = 16
WINDOW = 512
SEL_QBLOCK = 64
WIN_QBLOCK = 128
N_KV_STREAMS = 4
REL_BUCKETS = 32
REL_MAX_DIST = 2048
PEER_HEADS = 8
PEER_NKEYS = 128
PEER_EXPERTS = PEER_NKEYS * PEER_NKEYS
PEER_QDIM = 128
PEER_TOPK = 16
PEER_TBLOCK = 256

GDN_QK = GDN_HEADS * GDN_DK
GDN_V = GDN_HEADS * GDN_DV
GDN_CONV_CH = 2 * GDN_QK + GDN_V
NSA_Q = NSA_HEADS * NSA_HD
NSA_KV = NSA_KV_HEADS * NSA_HD
MIX_WIDTH = GDN_V + NSA_Q
OFF_CONV = 0
OFF_Z = OFF_CONV + GDN_CONV_CH
OFF_B = OFF_Z + GDN_V
OFF_A = OFF_B + GDN_HEADS
OFF_NQ = OFF_A + GDN_HEADS
OFF_NKV = OFF_NQ + NSA_Q
OFF_NWIN = OFF_NKV + N_KV_STREAMS * NSA_KV
OFF_NG = OFF_NWIN + 2 * NSA_KV
IN_DIM = OFF_NG + 3 * NSA_HEADS

kernel_name = 'hybrid_gdn_nsa_peer_step'

def rmsnorm(x, g):
    xf = x.astype(jnp.float32)
    y = xf * lax.rsqrt(jnp.mean(xf * xf, axis=-1, keepdims=True) + EPS)
    return (y * g.astype(jnp.float32)).astype(x.dtype)

def l2norm(x):
    xf = x.astype(jnp.float32)
    return (xf * lax.rsqrt(jnp.sum(xf * xf, axis=-1, keepdims=True) + EPS)).astype(x.dtype)

def masked_softmax(logits, valid):
    l = jnp.where(valid, logits.astype(jnp.float32), NEG_INF)
    m = jnp.max(l, axis=-1, keepdims=True)
    p = jnp.where(valid, jnp.exp(l - m), 0.0)
    return p / jnp.maximum(jnp.sum(p, axis=-1, keepdims=True), 1e-30)

def rel_bucket(dist):
    exact = REL_BUCKETS // 2
    d = jnp.maximum(dist, 0)
    df = jnp.maximum(d, 1).astype(jnp.float32)
    large = exact + (jnp.log(df / exact) / math.log(REL_MAX_DIST / exact)
                     * (REL_BUCKETS - exact)).astype(jnp.int32)
    large = jnp.minimum(large, REL_BUCKETS - 1)
    return jnp.where(d < exact, d, large)

def map_blocks(fn, xs, block, axis):
    n = xs[0].shape[axis]
    if n <= block:
        return fn(*xs)
    nb = -(-n // block)
    pad = nb * block - n

    def split(a):
        a = jnp.pad(a, [(0, pad) if i == axis else (0, 0) for i in range(a.ndim)])
        a = a.reshape(a.shape[:axis] + (nb, block) + a.shape[axis + 1:])
        return jnp.moveaxis(a, axis, 0)

    out = lax.map(lambda args: fn(*args), tuple(split(a) for a in xs))
    out = jnp.moveaxis(out, 0, axis)
    out = out.reshape(out.shape[:axis] + (nb * block,) + out.shape[axis + 2:])
    return lax.slice_in_dim(out, 0, n, axis=axis)

def causal_conv(xc, buf, w):
    L = xc.shape[1]
    xp = jnp.concatenate([buf.astype(xc.dtype), xc], axis=1)
    y = xp[:, 0:L] * w[0]
    for j in range(1, GDN_CONV):
        y = y + xp[:, j:j + L] * w[j]
    return jax.nn.silu(y), xp[:, L:]

def gated_delta_chunked(q, k, v, g, beta, s0):
    B, L, H, DK = q.shape
    C = GDN_CHUNK
    n = -(-L // C)
    pad = n * C - L

    def chunks(a):
        a = jnp.pad(a, [(0, 0), (0, pad)] + [(0, 0)] * (a.ndim - 2))
        a = a.reshape((B, n, C, H) + a.shape[3:])
        return jnp.moveaxis(a, 3, 2)

    qc, kc, vc, gc, bc = (chunks(a) for a in (q, k, v, g, beta))
    gc = jnp.cumsum(gc, axis=-1)
    causal = jnp.tril(jnp.ones((C, C), bool))
    strict = jnp.tril(jnp.ones((C, C), bool), -1)
    diff = gc[..., :, None] - gc[..., None, :]
    decay = jnp.where(causal, jnp.exp(jnp.where(causal, diff, 0.0)), 0.0)
    kb = kc * bc[..., None]
    lmat = jnp.where(strict, jnp.einsum('bnhid,bnhjd->bnhij', kb, kc) * decay, 0.0)
    eye = jnp.eye(C, dtype=jnp.float32)
    tmat = lax.linalg.triangular_solve(eye + lmat, jnp.broadcast_to(eye, lmat.shape),
                                       left_side=True, lower=True)
    u = tmat @ (vc * bc[..., None])
    w = tmat @ (kb * jnp.exp(gc)[..., None])
    a_intra = jnp.einsum('bnhid,bnhjd->bnhij', qc, kc) * decay
    q_dec = qc * jnp.exp(gc)[..., None]
    k_dec = kc * jnp.exp(gc[..., -1:] - gc)[..., None]
    g_last = jnp.exp(gc[..., -1])

    def step(s, xs):
        u_i, w_i, a_i, qd_i, kd_i, gl_i = xs
        v_new = u_i - w_i @ s
        o_i = qd_i @ s + a_i @ v_new
        s = s * gl_i[..., None, None] + jnp.swapaxes(kd_i, -1, -2) @ v_new
        return s, o_i

    xs = tuple(jnp.moveaxis(a, 1, 0) for a in (u, w, a_intra, q_dec, k_dec, g_last))
    s_fin, o = lax.scan(step, s0, xs)
    o = jnp.moveaxis(jnp.moveaxis(o, 0, 1), 2, 3).reshape(B, n * C, H, v.shape[-1])[:, :L]
    return o, s_fin

def nsa_compressed(q, qpos, k_all, v_all, rel_tab):
    B, Lp, G, D = k_all.shape
    Q = q.shape[1]
    nc = Lp // CMP_BLOCK
    kc = k_all.reshape(B, nc, CMP_BLOCK, G, D).mean(axis=2)
    vc = v_all.reshape(B, nc, CMP_BLOCK, G, D).mean(axis=2)
    dist = qpos[:, None] - (jnp.arange(nc) * CMP_BLOCK + CMP_BLOCK - 1)[None, :]
    bias = jnp.moveaxis(rel_tab[rel_bucket(dist)].reshape(Q, nc, G, NSA_GROUP), 1, 3)
    logits = jnp.einsum('bqgpd,bngd->bqgpn', q, kc).astype(jnp.float32) * (NSA_HD ** -0.5) + bias
    p = masked_softmax(logits, (dist >= 0)[:, None, None, :])
    o = jnp.einsum('bqgpn,bngd->bqgpd', p.astype(vc.dtype), vc)
    return o, p.sum(axis=3)

def select_blocks(imp, qpos):
    B, Q, G, nc = imp.shape
    nsb = nc * CMP_BLOCK // SEL_BLOCK
    score = imp.reshape(B, Q, G, nsb, SEL_BLOCK // CMP_BLOCK).sum(axis=-1)
    j = jnp.arange(nsb)[None, :]
    cur = (qpos // SEL_BLOCK)[:, None]
    forced = (j == 0) | (j == cur) | (j == cur - 1)
    future = j * SEL_BLOCK > qpos[:, None]
    score = jnp.where(future[:, None, :], -1.0, jnp.where(forced[:, None, :], FORCE_SCORE, score))
    _, idx = lax.top_k(score, min(SEL_TOPK, nsb))
    return idx

def nsa_selected(q, qpos, idx, k_all, v_all, rel_tab):
    B, Lp, G, D = k_all.shape
    Qb = q.shape[1]
    K = idx.shape[-1]
    nsb = Lp // SEL_BLOCK
    kb = k_all.reshape(B, nsb, SEL_BLOCK, G, D)
    vb = v_all.reshape(B, nsb, SEL_BLOCK, G, D)
    bi = jnp.arange(B)[:, None, None, None]
    gi = jnp.arange(G)[None, None, :, None]
    ksel = kb[bi, idx, :, gi, :]
    vsel = vb[bi, idx, :, gi, :]
    kpos = idx[..., None] * SEL_BLOCK + jnp.arange(SEL_BLOCK)
    dist = qpos[None, :, None, None, None] - kpos
    tab = rel_tab.reshape(REL_BUCKETS, G, NSA_GROUP)
    bias = tab[rel_bucket(dist), jnp.arange(G)[:, None, None]]
    bias = jnp.moveaxis(bias, -1, 3).reshape(B, Qb, G, NSA_GROUP, K * SEL_BLOCK)
    logits = jnp.einsum('bqgpd,bqgksd->bqgpks', q, ksel).astype(jnp.float32)
    logits = logits.reshape(B, Qb, G, NSA_GROUP, K * SEL_BLOCK) * (NSA_HD ** -0.5) + bias
    p = masked_softmax(logits, (dist >= 0).reshape(B, Qb, G, 1, K * SEL_BLOCK))
    return jnp.einsum('bqgpn,bqgnd->bqgpd', p.astype(vsel.dtype),
                      vsel.reshape(B, Qb, G, K * SEL_BLOCK, D))

def nsa_window(q, li, pos0, wb, k_seq, v_seq, rel_tab):
    Qb = q.shape[1]
    Lk = k_seq.shape[1]
    kw = wb + Qb
    start = jnp.minimum(li[0], Lk - kw)
    ks = lax.dynamic_slice_in_dim(k_seq, start, kw, axis=1)
    vs = lax.dynamic_slice_in_dim(v_seq, start, kw, axis=1)
    qpos = pos0 + li
    kpos = pos0 - wb + start + jnp.arange(kw)
    dist = qpos[:, None] - kpos[None, :]
    valid = (dist >= 0) & (dist <= WINDOW) & (kpos >= 0)[None, :]
    G = k_seq.shape[2]
    bias = jnp.moveaxis(rel_tab[rel_bucket(dist)].reshape(Qb, kw, G, NSA_GROUP), 1, 3)
    logits = jnp.einsum('bqgpd,bkgd->bqgpk', q, ks).astype(jnp.float32) * (NSA_HD ** -0.5) + bias
    p = masked_softmax(logits, valid[:, None, None, :])
    return jnp.einsum('bqgpk,bkgd->bqgpd', p.astype(vs.dtype), vs)

def peer(xn, w_q, sub_keys, u, v):
    B, L, dm = xn.shape
    xt = xn.reshape(B * L, dm)
    t = xt.shape[0]
    q = (xt @ w_q).reshape(t, PEER_HEADS, 2, PEER_QDIM // 2)
    s = jnp.einsum('thcd,hcnd->thcn', q, sub_keys).astype(jnp.float32)
    s1, i1 = lax.top_k(s[:, :, 0], PEER_TOPK)
    s2, i2 = lax.top_k(s[:, :, 1], PEER_TOPK)
    cand = (s1[..., :, None] + s2[..., None, :]).reshape(t, PEER_HEADS, PEER_TOPK * PEER_TOPK)
    cand_id = (i1[..., :, None] * PEER_NKEYS + i2[..., None, :]).reshape(t, PEER_HEADS, PEER_TOPK * PEER_TOPK)
    top, pos = lax.top_k(cand, PEER_TOPK)
    eid = jnp.take_along_axis(cand_id, pos, axis=-1)
    gate = jax.nn.softmax(top, axis=-1)

    def experts(xb, eb, gb):
        act = jax.nn.gelu(jnp.einsum('td,thkd->thk', xb, u[eb]).astype(jnp.float32), approximate=False)
        return jnp.einsum('thk,thkd->td', (gb * act).astype(xb.dtype), v[eb])

    out = map_blocks(experts, (xt, eid, gate), PEER_TBLOCK, 0)
    return out.reshape(B, L, dm)

def decoder_layer(x, pos0, conv_buf, s0, kv_past, win_buf, rel_bias,
                  norm1, w_in, gdn_conv_w, gdn_a_log, gdn_dt_bias, gdn_norm,
                  nsa_q_norm, nsa_k_norm, w_o, norm2, peer_wq, peer_subkeys, peer_u, peer_v):
    B, L, _ = x.shape
    dt = x.dtype
    G, P, D = NSA_KV_HEADS, NSA_GROUP, NSA_HD
    xn = rmsnorm(x, norm1)
    h = xn @ w_in

    conv_out, new_conv = causal_conv(h[..., OFF_CONV:OFF_Z], conv_buf, gdn_conv_w)
    qg = l2norm(conv_out[..., :GDN_QK].reshape(B, L, GDN_HEADS, GDN_DK)) * (GDN_DK ** -0.5)
    kg = l2norm(conv_out[..., GDN_QK:2 * GDN_QK].reshape(B, L, GDN_HEADS, GDN_DK))
    vg = conv_out[..., 2 * GDN_QK:].reshape(B, L, GDN_HEADS, GDN_DV)
    beta = jax.nn.sigmoid(h[..., OFF_B:OFF_A].astype(jnp.float32))
    gdec = -jnp.exp(gdn_a_log.astype(jnp.float32)) * jax.nn.softplus(
        h[..., OFF_A:OFF_NQ].astype(jnp.float32) + gdn_dt_bias.astype(jnp.float32))
    o_g, s_new = gated_delta_chunked(qg.astype(jnp.float32), kg.astype(jnp.float32),
                                     vg.astype(jnp.float32), gdec, beta, s0.astype(jnp.float32))
    z = h[..., OFF_Z:OFF_B].reshape(B, L, GDN_HEADS, GDN_DV).astype(jnp.float32)
    o_g = (rmsnorm(o_g, gdn_norm) * jax.nn.silu(z)).reshape(B, L, GDN_V).astype(dt)

    li = jnp.arange(L, dtype=jnp.int32)[None]
    qpos = pos0 + li[0]
    qn = rmsnorm(h[..., OFF_NQ:OFF_NKV].reshape(B, L, NSA_HEADS, D), nsa_q_norm).reshape(B, L, G, P, D)
    raw = h[..., OFF_NKV:OFF_NWIN].reshape(B, L, N_KV_STREAMS, G, D)
    kv_new = jnp.stack([rmsnorm(raw[:, :, 0], nsa_k_norm[0]), raw[:, :, 1],
                        rmsnorm(raw[:, :, 2], nsa_k_norm[1]), raw[:, :, 3]], axis=2)
    raw_w = h[..., OFF_NWIN:OFF_NG].reshape(B, L, 2, G, D)
    win_new = jnp.stack([rmsnorm(raw_w[:, :, 0], nsa_k_norm[2]), raw_w[:, :, 1]], axis=2)
    gates = jax.nn.sigmoid(h[..., OFF_NG:].reshape(B, L, G, P, 3).astype(jnp.float32))

    lt = kv_past.shape[1] + L
    pad = -(-lt // SEL_BLOCK) * SEL_BLOCK - lt
    kv_all = jnp.concatenate([kv_past.astype(dt), kv_new,
                              jnp.zeros((B, pad, N_KV_STREAMS, G, D), dt)], axis=1)
    o_cmp, imp = nsa_compressed(qn, qpos, kv_all[:, :, 0], kv_all[:, :, 1], rel_bias)
    idx = select_blocks(imp, qpos)
    ks_all, vs_all = kv_all[:, :, 2], kv_all[:, :, 3]
    o_slc = map_blocks(lambda qb, ib, lb: nsa_selected(qb, pos0 + lb[0], ib, ks_all, vs_all, rel_bias),
                       (qn, idx, li), SEL_QBLOCK, 1)
    wseq = jnp.concatenate([win_buf.astype(dt), win_new], axis=1)
    wb = win_buf.shape[1]
    wk, wv = wseq[:, :, 0], wseq[:, :, 1]
    o_win = map_blocks(lambda qb, lb: nsa_window(qb, lb[0], pos0, wb, wk, wv, rel_bias),
                       (qn, li), WIN_QBLOCK, 1)
    new_win = wseq[:, wseq.shape[1] - wb:]
    o_n = (gates[..., 0:1] * o_cmp + gates[..., 1:2] * o_slc + gates[..., 2:3] * o_win)
    o_n = o_n.reshape(B, L, NSA_Q).astype(dt)

    hres = x + jnp.concatenate([o_g, o_n], axis=-1) @ w_o
    y = hres + peer(rmsnorm(hres, norm2), peer_wq, peer_subkeys, peer_u, peer_v)
    return y, kv_new, new_win, new_conv, s_new.astype(dt)

def setup_inputs(seed: int = 0) -> dict:
    key = jax.random.key(seed)
    ks = jax.random.split(key, 24)
    n_pages = PAST_LEN // PAGE_SIZE
    n_used = DEC_BATCH * n_pages
    n_pool = n_used + n_used // 4
    win_rows = min(WINDOW, PAST_LEN)

    def normal(k, shape, scale):
        return jax.random.normal(k, shape, jnp.float32) * scale

    def gain(k, shape):
        return 1.0 + 0.02 * jax.random.normal(k, shape, jnp.float32)

    page_table = jax.random.permutation(ks[3], n_pool)[:n_used].reshape(DEC_BATCH, n_pages).astype(jnp.int32)
    dt_init = jnp.exp(jax.random.uniform(ks[9], (DEPTH, GDN_HEADS), jnp.float32,
                                         math.log(1e-3), math.log(1e-1)))
    return {
        'x_prompt': normal(ks[0], (BATCH, SEQ, D_MODEL), 1.0),
        'x_sample': normal(ks[1], (DEC_BATCH, DEC_SEQ, D_MODEL), 1.0),
        'cache_nsa_kv': normal(ks[2], (DEPTH, n_pool, PAGE_SIZE, N_KV_STREAMS, NSA_KV_HEADS, NSA_HD), 1.0),
        'page_table': page_table,
        'state_win_kv': normal(ks[4], (DEPTH, DEC_BATCH, win_rows, 2, NSA_KV_HEADS, NSA_HD), 1.0),
        'state_conv': normal(ks[5], (DEPTH, DEC_BATCH, GDN_CONV - 1, GDN_CONV_CH), 1.0),
        'state_gdn': normal(ks[6], (DEPTH, DEC_BATCH, GDN_HEADS, GDN_DK, GDN_DV), 0.5),
        'norm1': gain(ks[7], (DEPTH, D_MODEL)),
        'w_in': normal(ks[10], (DEPTH, D_MODEL, IN_DIM), D_MODEL ** -0.5),
        'gdn_conv_w': normal(ks[11], (DEPTH, GDN_CONV, GDN_CONV_CH), 0.5),
        'gdn_a_log': jnp.log(jax.random.uniform(ks[8], (DEPTH, GDN_HEADS), jnp.float32, 1.0, 16.0)),
        'gdn_dt_bias': jnp.log(jnp.expm1(dt_init)),
        'gdn_norm': gain(ks[12], (DEPTH, GDN_DV)),
        'nsa_q_norm': gain(ks[13], (DEPTH, NSA_HD)),
        'nsa_k_norm': gain(ks[14], (DEPTH, 3, NSA_HD)),
        'rel_bias': normal(ks[15], (REL_BUCKETS, NSA_HEADS), 0.5),
        'w_o': normal(ks[16], (DEPTH, MIX_WIDTH, D_MODEL), MIX_WIDTH ** -0.5),
        'norm2': gain(ks[17], (DEPTH, D_MODEL)),
        'peer_wq': normal(ks[18], (DEPTH, D_MODEL, PEER_HEADS * PEER_QDIM), D_MODEL ** -0.5),
        'peer_subkeys': normal(ks[19], (DEPTH, PEER_HEADS, 2, PEER_NKEYS, PEER_QDIM // 2), (PEER_QDIM // 2) ** -0.5),
        'peer_u': normal(ks[20], (DEPTH, PEER_EXPERTS, D_MODEL), D_MODEL ** -0.5),
        'peer_v': normal(ks[21], (DEPTH, PEER_EXPERTS, D_MODEL), 0.5),
    }

def reference(x_prompt, x_sample, cache_nsa_kv, page_table, state_win_kv, state_conv, state_gdn,
              norm1, w_in, gdn_conv_w, gdn_a_log, gdn_dt_bias, gdn_norm, nsa_q_norm, nsa_k_norm,
              rel_bias, w_o, norm2, peer_wq, peer_subkeys, peer_u, peer_v):
    b = x_prompt.shape[0]
    db = x_sample.shape[0]
    n_pages = page_table.shape[1]
    past_len = n_pages * cache_nsa_kv.shape[2]
    dt = x_prompt.dtype
    kv_tail = (N_KV_STREAMS, NSA_KV_HEADS, NSA_HD)
    y_prompt, y_sample = x_prompt, x_sample
    kvp_l, winp_l, convp_l, gdnp_l = [], [], [], []
    kvs_l, wins_l, convs_l, gdns_l = [], [], [], []
    for l in range(DEPTH):
        lw = (norm1[l], w_in[l], gdn_conv_w[l], gdn_a_log[l], gdn_dt_bias[l], gdn_norm[l],
              nsa_q_norm[l], nsa_k_norm[l], w_o[l], norm2[l], peer_wq[l], peer_subkeys[l],
              peer_u[l], peer_v[l])
        y_prompt, kvp, winp, convp, gdnp = decoder_layer(
            y_prompt, 0,
            jnp.zeros((b, GDN_CONV - 1, GDN_CONV_CH), dt),
            jnp.zeros((b, GDN_HEADS, GDN_DK, GDN_DV), dt),
            jnp.zeros((b, 0) + kv_tail, dt),
            jnp.zeros((b, WINDOW, 2, NSA_KV_HEADS, NSA_HD), dt),
            rel_bias, *lw)
        kv_past = cache_nsa_kv[l][page_table].reshape((db, past_len) + kv_tail)
        y_sample, kvs, wins, convs, gdns = decoder_layer(
            y_sample, past_len, state_conv[l], state_gdn[l], kv_past, state_win_kv[l],
            rel_bias, *lw)
        kvp_l.append(kvp); winp_l.append(winp); convp_l.append(convp); gdnp_l.append(gdnp)
        kvs_l.append(kvs); wins_l.append(wins); convs_l.append(convs); gdns_l.append(gdns)
    kv_rows_prompt = jnp.stack(kvp_l)
    win_prompt = jnp.stack(winp_l)
    conv_prompt = jnp.stack(convp_l)
    gdn_prompt = jnp.stack(gdnp_l)
    kv_rows_sample = jnp.stack(kvs_l)
    win_sample = jnp.stack(wins_l)
    conv_sample = jnp.stack(convs_l)
    gdn_sample = jnp.stack(gdns_l)
    return (y_prompt, y_sample, kv_rows_prompt, win_prompt, conv_prompt, gdn_prompt,
            kv_rows_sample, win_sample, conv_sample, gdn_sample)


_drawn_inputs = setup_inputs


def setup_inputs(seed=0):
    import zlib

    import numpy as np

    out = dict(_drawn_inputs(seed))
    spreads = {}
    factors = {'gdn_norm': 2.711, 'nsa_q_norm': 5.867, 'nsa_k_norm': 4.154}
    for name, (base, spread) in spreads.items():
        noise = np.random.default_rng([zlib.crc32(name.encode()), seed]).standard_normal(out[name].shape)
        drawn = base * np.exp(spread * noise) if base else spread * noise
        out[name] = jnp.asarray(drawn.astype(out[name].dtype))
    for name, factor in factors.items():
        out[name] = (out[name] * factor).astype(out[name].dtype)
    return out
```

```python
from contextlib import ExitStack
import math

import numpy as np

import concourse.bass as bass
from concourse import mybir

F32 = mybir.dt.float32
BF16 = mybir.dt.bfloat16
U32 = mybir.dt.uint32
I32 = mybir.dt.int32
ALU = mybir.AluOpType
ACT = mybir.ActivationFunctionType
AX = mybir.AxisListType

P = 128
D_MODEL = 1024
KD = D_MODEL // P
SEQ = 512
DEC_BATCH = 8
DEC_SEQ = 4
NSAMP = DEC_BATCH * DEC_SEQ
TOK = SEQ + NSAMP
TILES = SEQ // P + 1
ROWS = [P] * (TILES - 1) + [NSAMP]
EPS = 1e-6
NEG = -1e30

GH = 4
CONV_CH = 1536
CT = CONV_CH // P
TAPS = 4
COLS = 1824
C_Z, C_B, C_A, C_NQ, C_KV, C_WIN, C_G = 0, 512, 516, 520, 1032, 1544, 1800
IN_DIM = CONV_CH + COLS
CP = TAPS - 1 + SEQ
CS = TAPS - 1 + DEC_SEQ
CW = CP + DEC_BATCH * CS


class Chain:

    def __init__(self, eng, sem):
        self.eng, self.sem, self.n = eng, sem, 0

    def __call__(self, ins):
        self.n += 1
        ins.then_inc(self.sem, 1)
        self.eng.wait_ge(self.sem, self.n)


class Shared:
    pass


class scope:

    def __init__(self, nc, ctx, tag):
        self.nc, self.ctx, self.tag, self.sems = nc, ctx, tag, []
        ctx.callback(self.close)

    def sb(self, name, shape, dtype=F32):
        return self.ctx.enter_context(self.nc.sbuf_tensor(f"{self.tag}_{name}", shape, dtype))

    def ps(self, name, shape, dtype=F32):
        return self.ctx.enter_context(self.nc.psum_tensor(f"{self.tag}_{name}", shape, dtype))

    def sem(self, name):
        self.sems.append(self.nc.alloc_semaphore(f"{self.tag}_{name}"))
        return self.sems[-1]

    def close(self):
        if self.sems:
            self.nc.clear_and_free_semaphores(self.sems)
            self.nc.all_engine_barrier()


def project_stage(nc, I, O, S):
    with ExitStack() as ctx:
        a = scope(nc, ctx, "pj")
        x = a.sb("x", [P, 2, D_MODEL])
        junk = a.sb("junk", [P, D_MODEL], BF16)
        gain = a.sb("gain", [P, D_MODEL])
        xnT = S.mixT
        w_tok = a.sb("w_tok", [P, KD, COLS])
        w_conv = a.sb("w_conv", [P, 2, KD, 512])
        xs = a.sb("xs", [P, 2, D_MODEL])
        sq = a.sb("sq", [P, TILES])
        ms = a.sb("ms", [P, TILES])
        rt = a.sb("rt", [P, TILES])
        rstd = a.sb("rstd", [P, TILES])
        tp = [a.ps(f"tp{i}", [P, 4, P]) for i in range(2)]
        acc = [a.ps(f"acc{i}", [P, 512]) for i in range(4)]
        accs = [a.ps(f"accs{i}", [P, 512]) for i in range(2)]

        x_in = [a.sem(f"x_in{i}") for i in range(2)]
        gain_in = a.sem("gain_in")
        w_in = a.sem("w_in")
        wc_in = [a.sem(f"wc_in{i}") for i in range(2)]
        ident_ok = a.sem("ident_ok")
        ms_ok, root_ok, sq_ok = a.sem("ms_ok"), a.sem("root_ok"), a.sem("sq_ok")
        rstd_ok, xs_ok = a.sem("rstd_ok"), a.sem("xs_ok")
        tp_ok, tp_used = a.sem("tp_ok"), a.sem("tp_used")
        mm_ok = a.sem("mm_ok")
        out_a, out_v = a.sem("out_a"), a.sem("out_v")
        samp_out = a.sem("samp_out")
        pad_ok = a.sem("pad_ok")

        jobs = [("t", m, c) for m in range(TILES) for c in range(0, COLS, 512)]
        jobs += [("c", 0, c) for c in range(CT)]

        def x_rows(m):
            return I["x_prompt"][0, m * P:(m + 1) * P, :] if m < TILES - 1 else \
                I["x_sample"].rearrange("b t d -> (b t) d")

        block = ctx.enter_context(nc.Block())

        @block.sync
        def _(sp):
            w = I["w_in"][0].rearrange("(k p) n -> p k n", p=P)
            for m in range(2):
                sp.dma_start(x[0:ROWS[m], m % 2, :], x_rows(m)).then_inc(x_in[m % 2], 16)
            sp.dma_start(gain[:, :], I["norm1"].to_broadcast([P, D_MODEL])).then_inc(gain_in, 16)
            for k in range(KD):
                sp.dma_start(w_tok[:, k, :], w[:, k, CONV_CH:IN_DIM]).then_inc(w_in, 16)
            for m in range(2, TILES):
                sp.wait_ge(xs_ok, m - 1)
                sp.dma_start(x[0:ROWS[m], m % 2, :], x_rows(m)).then_inc(x_in[m % 2], 16)
            for n in range(CT // 4):
                if n >= 2:
                    sp.wait_ge(mm_ok, len(jobs) - CT + 4 * (n - 1))
                sp.dma_start(w_conv[:, n % 2, :, :], w[:, :, 512 * n:512 * n + 512]).then_inc(wc_in[n % 2], 16)

        @block.gpsimd
        def _(pool):
            pool.memset(S.ident[:, :], 0.0).then_inc(ident_ok, 1)
            pool.wait_ge(ident_ok, 1)
            pool.affine_select(out=S.ident[:, :], in_=S.ident[:, :], compare_op=ALU.not_equal, fill=1.0,
                               base=0, pattern=[[-1, P]], channel_multiplier=1).then_inc(ident_ok, 1)
            pool.memset(S.conv_in[:, :, 0:TAPS - 1], 0.0).then_inc(pad_ok, 1)

        @block.scalar
        def _(act):
            for m in range(TILES):
                r = ROWS[m]
                act.wait_ge(x_in[m % 2], 16 * (m // 2 + 1))
                if m >= 1:
                    act.wait_ge(sq_ok, m)
                act.activation(junk[0:r, :], x[0:r, m % 2, :], ACT.Square,
                               accum_out=sq[0:r, m:m + 1]).then_inc(sq_ok, 1)
                act.wait_ge(ms_ok, m + 1)
                act.activation(rt[0:r, m:m + 1], ms[0:r, m:m + 1], ACT.Sqrt).then_inc(root_ok, 1)
            for j, (kind, m, c) in enumerate(jobs):
                if j % 2 == 0:
                    act.wait_ge(mm_ok, j + 1)
                    if kind == "t":
                        n = min(512, COLS - c)
                        act.activation(S.h_tok[0:ROWS[m], m, c:c + n], acc[j % 4][0:ROWS[m], 0:n],
                                       ACT.Copy).then_inc(out_a, 1)
                    else:
                        act.activation(S.conv_in[:, c, TAPS - 1:CP], acc[j % 4][:, :], ACT.Copy)\
                            .then_inc(out_a, 1)

        @block.vector
        def _(dve):
            for m in range(TILES):
                r = ROWS[m]
                dve.wait_ge(sq_ok, m + 1)
                dve.tensor_scalar(ms[0:r, m:m + 1], sq[0:r, m:m + 1], 1.0 / D_MODEL, EPS, ALU.mult,
                                  ALU.add).then_inc(ms_ok, 1)
                dve.wait_ge(root_ok, m + 1)
                dve.reciprocal(rstd[0:r, m:m + 1], rt[0:r, m:m + 1]).then_inc(rstd_ok, 1)
                dve.wait_ge(rstd_ok, m + 1)
                if m == 0:
                    dve.wait_ge(gain_in, 16)
                dve.scalar_tensor_tensor(out=xs[0:r, m % 2, :], in0=x[0:r, m % 2, :],
                                         scalar=rstd[0:r, m:m + 1], in1=gain[0:r, :],
                                         op0=ALU.mult, op1=ALU.mult).then_inc(xs_ok, 1)
                for g in range(2):
                    n = 2 * m + g
                    dve.wait_ge(tp_ok, n + 1)
                    dve.tensor_copy(xnT[:, 4 * g:4 * g + 4, m * P:m * P + r],
                                    tp[n % 2][:, :, 0:r]).then_inc(tp_used, 1)
            for j, (kind, m, c) in enumerate(jobs):
                if kind == "t" and j % 2 == 1:
                    dve.wait_ge(mm_ok, j + 1)
                    n = min(512, COLS - c)
                    dve.tensor_copy(S.h_tok[0:ROWS[m], m, c:c + n],
                                    acc[j % 4][0:ROWS[m], 0:n]).then_inc(out_v, 1)
                if kind == "c":
                    dve.wait_ge(mm_ok, j + 1)
                    if j % 2 == 1:
                        dve.tensor_copy(S.conv_in[:, c, TAPS - 1:CP], acc[j % 4][:, :]).then_inc(out_v, 1)
                    dst = S.conv_in[:, c, CP:CW].rearrange("p (b s) -> p b s", s=CS)[:, :, TAPS - 1:CS]
                    dve.tensor_copy(dst, accs[j % 2][:, 0:NSAMP].rearrange("p (b t) -> p b t", t=DEC_SEQ))\
                        .then_inc(samp_out, 1)

        @block.tensor
        def _(pe):
            pe.wait_ge(ident_ok, 2)
            for m in range(TILES):
                r = ROWS[m]
                pe.wait_ge(xs_ok, m + 1)
                for g in range(2):
                    n = 2 * m + g
                    if n >= 2:
                        pe.wait_ge(tp_used, n - 1)
                    for k in range(4):
                        mm = pe.transpose(tp[n % 2][:, k, 0:r],
                                          xs[0:r, m % 2, (4 * g + k) * P:(4 * g + k + 1) * P],
                                          S.ident[0:r, 0:r])
                    mm.then_inc(tp_ok, 1)
            pe.wait_ge(tp_used, 2 * TILES)
            for j, (kind, m, c) in enumerate(jobs):
                if j >= 4:
                    pe.wait_ge(out_v if j % 2 else out_a, (j - 4) // 2 + 1)
                if kind == "t":
                    n = min(512, COLS - c)
                    for k in range(KD):
                        if j == 0:
                            pe.wait_ge(w_in, 16 * KD)
                        mm = pe.matmul(acc[j % 4][0:ROWS[m], 0:n], xnT[:, k, m * P:m * P + ROWS[m]],
                                       w_tok[:, k, c:c + n], start=(k == 0), stop=(k == KD - 1))
                    mm.then_inc(mm_ok, 1)
                else:
                    n = c // 4
                    if c % 4 == 0:
                        pe.wait_ge(wc_in[n % 2], 16 * (n // 2 + 1))
                    if c >= 2:
                        pe.wait_ge(samp_out, c - 1)
                    for k in range(KD):
                        w = w_conv[:, n % 2, k, c % 4 * P:(c % 4 + 1) * P]
                        pe.matmul(accs[j % 2][:, 0:NSAMP], w, xnT[:, k, SEQ:TOK],
                                  start=(k == 0), stop=(k == KD - 1))
                        mm = pe.matmul(acc[j % 4][:, :], w, xnT[:, k, 0:SEQ],
                                       start=(k == 0), stop=(k == KD - 1))
                    mm.then_inc(mm_ok, 1)


LEVELS = int(math.log2(P))
SAMPLE_LEVELS = int(math.log2(DEC_SEQ))


def masks_stage(nc, I, O, S):
    with ExitStack() as ctx:
        a = scope(nc, ctx, "mk")
        col = a.sb("col", [P, P], I32)
        row = a.sb("row", [P, 1], I32)
        cs = a.sb("cs", [P, P], I32)
        rs = a.sb("rs", [P, 1], I32)
        rf = a.sb("rf", [P, 1])
        same = a.sb("same", [P, LEVELS + 1, P])
        low = a.sb("low", [P, P])
        iota_ok, done = a.sem("iota_ok"), a.sem("done")
        low_ok = a.sem("low_ok")
        pool_chain, dve_chain = a.sem("pool_chain"), a.sem("dve_chain")
        block = ctx.enter_context(nc.Block())

        @block.gpsimd
        def _(pool):
            step = Chain(pool, pool_chain)
            pool.iota(col[:, :], [[1, P]], base=0, channel_multiplier=0).then_inc(iota_ok, 1)
            pool.iota(row[:, :], [[0, 1]], base=0, channel_multiplier=1).then_inc(iota_ok, 1)
            step(pool.memset(S.ones[:, :], 1.0))
            step(pool.memset(low[:, :], 0.0))
            step(pool.memset(S.ident[:, :], 0.0))
            step(pool.affine_select(out=S.ident[:, :], in_=S.ident[:, :], compare_op=ALU.not_equal, fill=1.0,
                                    base=0, pattern=[[-1, P]], channel_multiplier=1))
            step(pool.affine_select(out=S.upper[:, :], in_=S.ones[:, :], compare_op=ALU.is_ge, fill=0.0,
                                    base=0, pattern=[[1, P]], channel_multiplier=-1))
            step(pool.affine_select(out=S.neg_strict[:, :], in_=low[:, :], compare_op=ALU.is_gt, fill=NEG,
                                    base=0, pattern=[[-1, P]], channel_multiplier=1))
            pool.affine_select(out=S.neg_upper[:, :], in_=low[:, :], compare_op=ALU.is_ge, fill=NEG,
                               base=0, pattern=[[1, P]], channel_multiplier=-1).then_inc(low_ok, 1)

        @block.vector
        def _(dve):
            step = Chain(dve, dve_chain)
            dve.wait_ge(iota_ok, 2)
            for lv in range(LEVELS + 1):
                if lv == LEVELS:
                    step(dve.memset(same[:, lv, :], 1.0))
                    continue
                if lv == 0:
                    step(dve.tensor_copy(rf[:, :], row[:, :]))
                    step(dve.tensor_scalar(same[:, lv, :], col[:, :], rf[:, 0:1], None, ALU.is_equal))
                    continue
                step(dve.tensor_scalar(cs[:, :], col[:, :], lv, None, ALU.arith_shift_right))
                step(dve.tensor_scalar(rs[:, :], row[:, :], lv, None, ALU.arith_shift_right))
                step(dve.tensor_copy(rf[:, :], rs[:, :]))
                step(dve.tensor_scalar(same[:, lv, :], cs[:, :], rf[:, 0:1], None, ALU.is_equal))
            for lv in range(LEVELS):
                step(dve.tensor_tensor(S.join[:, lv, :], same[:, lv + 1, :], same[:, lv, :], ALU.subtract))
            n = NSAMP
            sq = same[0:n, SAMPLE_LEVELS, 0:n]
            dve.wait_ge(low_ok, 1)
            step(dve.tensor_copy(S.seq_ones[:, :], sq))
            step(dve.tensor_tensor(S.seq_upper[:, :], sq, S.upper[0:n, 0:n], ALU.mult))
            step(dve.tensor_scalar(low[0:n, 0:n], sq, 1.0, -NEG, ALU.subtract, ALU.mult))
            step(dve.tensor_tensor(S.seq_neg_strict[:, :], low[0:n, 0:n], S.neg_strict[0:n, 0:n], ALU.min))
            step(dve.tensor_tensor(S.seq_neg_upper[:, :], low[0:n, 0:n], S.neg_upper[0:n, 0:n], ALU.min))
            step(dve.memset(S.mean[:, :], 0.0))
            step(dve.tensor_scalar(S.mean[:, CB - 4:CB], same[:, 5, 0:P:32], 1.0 / 32, None, ALU.mult))
            for m in range(TILES - 1):
                step(dve.tensor_copy(S.mean_rep[:, m, :].rearrange("p (h n) -> p h n", h=8),
                                     S.mean[:, CB - 4 - 4 * m:CB - 4 - 4 * m + 16].unsqueeze(1)
                                     .to_broadcast([P, 8, 16])))
            step(dve.tensor_copy(S.head_rows[:, :], same[:, 4, 0:P:16]))
            step(dve.tensor_scalar(S.other_seq[:, :], same[:, 5, 0:P:32], 1.0, -NEG, ALU.subtract, ALU.mult))
            step(dve.tensor_scalar(rs[:, :], row[:, :], 3, None, ALU.bitwise_and))
            step(dve.tensor_copy(rf[:, :], rs[:, :]))
            step(dve.tensor_scalar(cs[:, :], col[:, :], 3, None, ALU.bitwise_and))
            step(dve.tensor_scalar(S.peers[:, :], cs[:, :], rf[:, 0:1], None, ALU.is_equal))
            step(dve.tensor_tensor(S.peers[:, :], S.peers[:, :], same[:, 4, :], ALU.mult))
            step(dve.tensor_scalar(rs[:, :], row[:, :], 16, 4, ALU.bitwise_and, ALU.logical_shift_right))
            step(dve.tensor_copy(S.in_group[:, 1:2], rs[:, :]))
            step(dve.tensor_scalar(S.in_group[:, 0:1], S.in_group[:, 1:2], -1.0, 1.0, ALU.mult, ALU.add))
            step(dve.tensor_copy(S.index16[:, :], col[:, 0:16]))
            step(dve.tensor_copy(S.seq_pick[:, :], same[0:n, SAMPLE_LEVELS, 0:n:DEC_SEQ]))


def conv_stage(nc, I, O, S):
    TAIL = 3 + DEC_BATCH * 3
    W = CW - 3
    with ExitStack() as ctx:
        a = scope(nc, ctx, "cv")
        rows28 = a.sb("rows28", [TAPS + DEC_BATCH * 3, CONV_CH])
        cw = a.sb("cw", [P, CT, TAPS])
        tmp = a.sb("tmp", [P, 2, CW])
        sqs = a.sb("sqs", [P, 8, TOK])
        tail_c = a.sb("tail_c", [P, CT, TAIL])
        tail_r = a.sb("tail_r", [TAIL, CONV_CH])
        p_rows = a.ps("p_rows", [P, CT, 32])
        p_tail = [a.ps(f"p_tail{i}", [P, 4, P]) for i in range(3)]
        p_nrm = a.ps("p_nrm", [P, TILES, 8])
        rows_in, rows_T, cw_ok, state_ok = (a.sem(n) for n in ("rows_in", "rows_T", "cw_ok", "state_ok"))
        first_ok, taps_ok, silu_ok, sq_ok, nrm_ok = (
            a.sem(n) for n in ("first_ok", "taps_ok", "silu_ok", "sq_ok", "nrm_ok"))
        tailc_ok, tail_T, tailr_ok, stored = (a.sem(n) for n in ("tailc_ok", "tail_T", "tailr_ok", "stored"))
        chain = a.sem("chain")
        block = ctx.enter_context(nc.Block())

        @block.sync
        def _(sp):
            sp.dma_start(rows28[0:TAPS, :], I["gdn_conv_w"][0]).then_inc(rows_in, 16)
            sp.dma_start(rows28[TAPS:, :], I["state_conv"][0].rearrange("b s c -> (b s) c"))\
                .then_inc(rows_in, 16)
            sp.wait_ge(tailr_ok, 3)
            sp.dma_start(O["conv_prompt"][0, 0], tail_r[0:3, :]).then_inc(stored, 16)
            sp.dma_start(O["conv_sample"][0].rearrange("b s c -> (b s) c"), tail_r[3:TAIL, :])\
                .then_inc(stored, 16)
            sp.wait_ge(stored, 32)

        @block.tensor
        def _(pe):
            pe.wait_ge(rows_in, 32)
            n = TAPS + DEC_BATCH * 3
            for c in range(CT):
                mm = pe.transpose(p_rows[:, c, 0:n], rows28[:, c * P:(c + 1) * P], S.ident[0:n, 0:n])
            mm.then_inc(rows_T, 1)
            pe.wait_ge(tailc_ok, 2)
            for g in range(3):
                for c in range(4):
                    mm = pe.transpose(p_tail[g][0:TAIL, c, :], tail_c[:, 4 * g + c, :], S.ident[:, :])
                mm.then_inc(tail_T, 1)
            for c in range(8):
                pe.wait_ge(sq_ok, c + 1)
                for m in range(TILES):
                    mm = pe.matmul(p_nrm[0:ROWS[m], m, c:c + 1], sqs[:, c, m * P:m * P + ROWS[m]],
                                   S.ones[:, 0:1], start=True, stop=True)
            mm.then_inc(nrm_ok, 1)

        @block.vector
        def _(dve):
            dve.wait_ge(rows_T, 1)
            dve.tensor_copy(cw[:, :, :], p_rows[:, :, 0:TAPS]).then_inc(cw_ok, 1)
            state = S.conv_in[:, :, CP:CW].rearrange("p c (b s) -> p c b s", s=CS)
            for b in range(DEC_BATCH):
                last = dve.tensor_copy(state[:, :, b, 0:3], p_rows[:, :, TAPS + 3 * b:TAPS + 3 * b + 3])
            last.then_inc(state_ok, 1)
            dve.wait_ge(state_ok, 1)
            dve.tensor_copy(tail_c[:, :, 0:3], S.conv_in[:, :, SEQ:SEQ + 3]).then_inc(tailc_ok, 1)
            for b in range(DEC_BATCH):
                last = dve.tensor_copy(tail_c[:, :, 3 + 3 * b:6 + 3 * b], state[:, :, b, DEC_SEQ:CS])
            last.then_inc(tailc_ok, 1)
            step = Chain(dve, chain)
            for c in range(CT):
                dve.wait_ge(first_ok, c + 1)
                for j in range(1, TAPS):
                    ins = dve.scalar_tensor_tensor(out=tmp[:, c % 2, 0:W], in0=S.conv_in[:, c, j:j + W],
                                                   scalar=cw[:, c, j:j + 1], in1=tmp[:, c % 2, 0:W],
                                                   op0=ALU.mult, op1=ALU.add)
                    if j < TAPS - 1:
                        step(ins)
                ins.then_inc(taps_ok, 1)
            for g in range(3):
                dve.wait_ge(tail_T, g + 1)
                dve.tensor_copy(tail_r[:, 512 * g:512 * g + 512],
                                p_tail[g][0:TAIL, :, :].rearrange("p c n -> p (c n)")).then_inc(tailr_ok, 1)
            dve.memset(S.nrm[:, :, :], 1.0).then_inc(nrm_ok, 1)
            dve.wait_ge(nrm_ok, 2)
            step(dve.tensor_copy(S.nrm[:, 0:TILES - 1, :], p_nrm[:, 0:TILES - 1, :]))
            step(dve.tensor_copy(S.nrm[0:NSAMP, TILES - 1, :], p_nrm[0:NSAMP, TILES - 1, :]))

        @block.scalar
        def _(act):
            act.wait_ge(cw_ok, 1)
            act.wait_ge(state_ok, 1)

            def silu(c):
                act.wait_ge(taps_ok, c + 1)
                act.activation(S.cs[:, c, 0:SEQ], tmp[:, c % 2, 0:SEQ], ACT.Silu).then_inc(silu_ok, 1)
                src = tmp[:, c % 2, CP:CW].rearrange("p (b s) -> p b s", s=CS)[:, :, 0:DEC_SEQ]
                act.activation(S.cs[:, c, SEQ:TOK].rearrange("p (b t) -> p b t", t=DEC_SEQ), src,
                               ACT.Silu).then_inc(silu_ok, 1)

            for c in range(CT):
                if c >= 2:
                    act.wait_ge(silu_ok, 2 * (c - 1))
                act.activation(tmp[:, c % 2, 0:W], S.conv_in[:, c, 0:W], ACT.Copy, scale=cw[:, c, 0:1])\
                    .then_inc(first_ok, 1)
                if c >= 1:
                    silu(c - 1)
            silu(CT - 1)
            for m in range(TILES):
                act.activation(S.zs[0:ROWS[m], m, :], S.h_tok[0:ROWS[m], m, C_Z:C_Z + 512], ACT.Silu)

        @block.gpsimd
        def _(pool):
            for c in range(8):
                pool.wait_ge(silu_ok, 2 * (c + 1))
                pool.tensor_tensor(sqs[:, c, :], S.cs[:, c, :], S.cs[:, c, :], ALU.mult).then_inc(sq_ok, 1)


def delta_stage(nc, I, O, S):
    NP = TILES - 1
    SM = TILES - 1
    QS = P ** -0.5
    with ExitStack() as ctx:
        a = scope(nc, ctx, "dl")
        gn = a.sb("gn", [P, P])
        alog, dtb, ea = (a.sb(n, [P, GH]) for n in ("alog", "dtb", "ea"))
        gb = a.sb("gb", [P, TILES, 8])
        v = {n: a.sb(n, [P, TILES, GH]) for n in
             "eb b1 beta xa ax ex spl xm g gcum ngc glast egc dk ek nbe rq ss rst".split()}
        rinv = a.sb("rinv", [P, TILES, 8])
        glS = a.sb("glS", [P, DEC_BATCH * GH])
        gsel = a.sb("gsel", [NSAMP, DEC_BATCH, GH])
        gl = a.sb("gl", [P, NP, GH])
        kn, knT, vb, aT, L, U, T = (a.sb(n, [P, TILES, GH, P]) for n in "kn knT vb aT L U T".split())
        LM = a.sb("LM", [P, 2, GH, P])
        Y = S.h_tok[:, 0:2, C_Z:C_Z + GH * P].rearrange("p x (h n) -> p x h n", h=GH)
        spare = S.mixT[:, GH:KD, :].rearrange("p c t -> p (c t)")
        dm, dt_ = (spare[:, i * 1024:(i + 1) * 1024].rearrange("p (x h n) -> p x h n", x=2, h=GH) for i in range(2))
        pb = [a.ps(f"pb{i}", [P, 4, P]) for i in range(8)]
        block = ctx.enter_context(nc.Block())
        bc = lambda x, r, n: x.unsqueeze(2).to_broadcast([r, GH, n])
        hb = lambda x, r, n: x.unsqueeze(1).to_broadcast([r, GH, n])
        kdx = lambda buf: buf[0:NSAMP, :, :, :].rearrange("p x h n -> p (x h) n")
        LMJ = a.sb("lmj", [P, P], BF16)
        st = S.h_tok[:, 2, C_Z:C_Z + GH * P].rearrange("p (h n) -> p h n", h=GH)
        flat, at = S.conv_in[:, :, :].rearrange("p c w -> p (c w)"), DEC_BATCH * GH * P
        s0 = flat[:, 0:at].rearrange("p (b h n) -> p b h n", b=DEC_BATCH, h=GH)
        kx, qx = (flat[:, at + i * 1024:at + (i + 1) * 1024].rearrange("p (h b n) -> p h b n", h=GH, b=DEC_BATCH)
                  for i in range(2))
        small_in, s0_in, stored = a.sem("small_in"), a.sem("s0_in"), a.sem("stored")
        dv_chain, pl_chain, ac_chain = a.sem("dv_chain"), a.sem("pl_chain"), a.sem("ac_chain")
        (nrm_e, root_ok, gates_in, exp_ok, g_ok, gc_mm, gc_ok, egc_ok, fac_ok) = (a.sem(n) for n in (
            "nrm_e", "root_ok", "gates_in", "exp_ok", "g_ok", "gc_mm", "gc_ok", "egc_ok", "fac_ok"))
        (kT_mm, kn_ok, vb_ok, knT_mm, knT_ok, gr_mm, diff_ok, dec_ok, kk_mm, l_ok, aT_ok, lb_ok) = (
            a.sem(n) for n in ("kT_mm", "kn_ok", "vb_ok", "knT_mm", "knT_ok", "gr_mm", "diff_ok", "dec_ok",
                               "kk_mm", "l_ok", "aT_ok", "lb_ok"))
        (lm_ok, lt_mm, ut_ok, y_mm, y_sb, uy_mm) = (a.sem(n) for n in (
            "lm_ok", "lt_mm", "ut_ok", "y_mm", "y_sb", "uy_mm"))
        (kd_ok, ks_mm, r_ok, vn_mm, vn_sb, ds_mm, st_ok, o1_ok, o_ok, yq_ok, ss_ok) = (a.sem(n) for n in (
            "kd_ok", "ks_mm", "r_ok", "vn_mm", "vn_sb", "ds_mm", "st_ok", "o1_ok", "o_ok", "yq_ok", "ss_ok"))
        (x_ok, kdx_ok, sds_mm, sst_ok, rst_ok, zg_ok, og_ok, ogT_mm, og_out) = (a.sem(n) for n in (
            "x_ok", "kdx_ok", "sds_mm", "sst_ok", "rst_ok", "zg_ok", "og_ok", "ogT_mm", "og_out"))
        items = [(lv, m) for lv in range(1, LEVELS) for m in (range(TILES) if lv < SAMPLE_LEVELS else range(NP))]
        before = [max([i for i in range(q) if items[i][1] == items[q][1]], default=None) if q else None
                  for q in range(len(items))]
        scan = list(range(NP)) + [SM]

        @block.sync
        def _(sp):
            sp.dma_start(gn[:, :], I["gdn_norm"].to_broadcast([P, P])).then_inc(small_in, 16)
            sp.dma_start(alog[:, :], I["gdn_a_log"].to_broadcast([P, GH])).then_inc(small_in, 16)
            sp.dma_start(dtb[:, :], I["gdn_dt_bias"].to_broadcast([P, GH])).then_inc(small_in, 16)
            sp.dma_start(s0[:, :, :, :], I["state_gdn"][0].rearrange("b h k v -> k b h v")).then_inc(s0_in, 16)
            sp.wait_ge(st_ok, NP * GH)
            sp.dma_start(O["gdn_prompt"][0, 0].rearrange("h k v -> k h v"), st[:, :, :]).then_inc(stored, 16)
            sp.wait_ge(sst_ok, GH * 2)
            sp.dma_start(O["gdn_sample"][0].rearrange("b h k v -> k b h v"), s0[:, :, :, :])\
                .then_inc(stored, 16)
            sp.wait_ge(stored, 32)

        @block.vector
        def _(dve):
            step = Chain(dve, dv_chain)
            dve.tensor_scalar(rinv[:, :, :], S.nrm[:, :, :], EPS, None, ALU.add).then_inc(nrm_e, 1)
            step(dve.memset(gb[:, :, :], 0.0))
            step(dve.tensor_copy(gb[:, 0:NP, :], S.h_tok[:, 0:NP, C_B:C_B + 8]))
            step(dve.tensor_copy(gb[0:NSAMP, SM, :], S.h_tok[0:NSAMP, SM, C_B:C_B + 8]))
            dve.wait_ge(small_in, 48)
            step(dve.tensor_tensor(v["xa"][:, :, :], gb[:, :, 4:8], dtb[:, :].unsqueeze(1).to_broadcast([P, TILES, GH]),
                                   ALU.add))
            step(dve.tensor_scalar(v["xm"][:, :, :], v["xa"][:, :, :], 0.0, None, ALU.max))
            dve.scalar_tensor_tensor(out=v["ax"][:, :, :], in0=v["xm"][:, :, :], scalar=-2.0, in1=v["xa"][:, :, :],
                                     op0=ALU.mult, op1=ALU.add).then_inc(gates_in, 1)
            dve.wait_ge(exp_ok, 4)
            dve.wait_ge(gates_in, 1)
            step(dve.tensor_scalar(v["b1"][:, :, :], v["eb"][:, :, :], 1.0, None, ALU.add))
            step(dve.reciprocal(v["beta"][:, :, :], v["b1"][:, :, :]))
            step(dve.tensor_tensor(v["spl"][:, :, :], v["spl"][:, :, :], v["xm"][:, :, :], ALU.add))
            step(dve.scalar_tensor_tensor(out=v["g"][:, :, :], in0=v["spl"][:, :, :], scalar=-1.0,
                                          in1=ea[:, :].unsqueeze(1).to_broadcast([P, TILES, GH]),
                                          op0=ALU.mult, op1=ALU.mult))
            for b in range(DEC_BATCH):
                last = dve.tensor_scalar(gsel[:, b, :], v["g"][0:NSAMP, SM, :], S.seq_pick[:, b:b + 1], None, ALU.mult)
            last.then_inc(g_ok, 1)
            dve.wait_ge(root_ok, 1)
            step(dve.reciprocal(rinv[:, :, :], rinv[:, :, :]))
            step(dve.tensor_scalar(v["rq"][:, :, :], rinv[:, :, 0:4], QS, None, ALU.mult))
            step(dve.memset(v["gcum"][:, :, :], 0.0))
            step(dve.memset(v["glast"][:, :, :], 0.0))
            dve.wait_ge(gc_mm, 1)
            sums = pb[5][:, 0, 0:TILES * 8].rearrange("p (m e) -> p m e", e=8)
            step(dve.tensor_copy(v["gcum"][:, 0:NP, :], sums[:, 0:NP, 0:4]))
            step(dve.tensor_copy(v["gcum"][0:NSAMP, SM, :], sums[0:NSAMP, SM, 0:4]))
            step(dve.tensor_copy(v["glast"][:, 0:NP, :], sums[:, 0:NP, 4:8]))
            step(dve.tensor_copy(v["glast"][0:NSAMP, SM, :], sums[0:NSAMP, SM, 4:8]))
            step(dve.tensor_copy(glS[:, :], pb[5][:, 1, 0:DEC_BATCH * GH]))
            step(dve.tensor_scalar(v["ngc"][:, :, :], v["gcum"][:, :, :], -1.0, None, ALU.mult))
            dve.tensor_tensor(v["dk"][:, :, :], v["glast"][:, :, :], v["gcum"][:, :, :], ALU.subtract).then_inc(gc_ok, 1)
            dve.wait_ge(egc_ok, 4)
            step(dve.scalar_tensor_tensor(out=v["nbe"][:, :, :], in0=v["beta"][:, :, :], scalar=-1.0,
                                          in1=v["egc"][:, :, :], op0=ALU.mult, op1=ALU.mult))
            dve.memset(v["ss"][:, :, :], 1.0).then_inc(fac_ok, 1)
            for m in range(TILES):
                r = ROWS[m]
                dve.wait_ge(kT_mm, m + 1)
                dve.tensor_tensor(kn[0:r, m, :, :], pb[0][0:r, :, :], bc(rinv[0:r, m, 4:8], r, P), ALU.mult)\
                    .then_inc(kn_ok, 1)
                dve.tensor_tensor(vb[0:r, m, :, :], pb[1][0:r, :, :], bc(v["beta"][0:r, m, :], r, P), ALU.mult)\
                    .then_inc(vb_ok, 1)
                dve.wait_ge(gr_mm, m + 1)
                if m >= 2:
                    dve.wait_ge(l_ok, 2 * (m - 1))
                gr = pb[2][0:r, :, 0:r]
                ns, nu = (S.neg_strict, S.neg_upper) if m < SM else (S.seq_neg_strict, S.seq_neg_upper)
                dve.tensor_tensor(dm[0:r, m % 2, :, 0:r], hb(ns[0:r, 0:r], r, r), gr, ALU.subtract)
                dve.tensor_tensor(dt_[0:r, m % 2, :, 0:r], hb(nu[0:r, 0:r], r, r), gr, ALU.add).then_inc(diff_ok, 1)
                dve.wait_ge(dec_ok, m + 1)
                dve.wait_ge(kk_mm, m + 1)
                dve.tensor_tensor(L[0:r, m, :, 0:r], pb[3][0:r, :, 0:r], dm[0:r, m % 2, :, 0:r], ALU.mult)\
                    .then_inc(l_ok, 1)
                dve.tensor_tensor(aT[0:r, m, :, 0:r], pb[4][0:r, :, 0:r], dt_[0:r, m % 2, :, 0:r], ALU.mult)\
                    .then_inc(l_ok, 1)
            for m in range(TILES):
                r = ROWS[m]
                dve.wait_ge(lt_mm, m + 1)
                dve.tensor_tensor(U[0:r, m, :, 0:r], hb(S.ident[0:r, 0:r], r, r), pb[m % 2][0:r, :, 0:r],
                                  ALU.subtract)
                dve.tensor_tensor(T[0:r, m, :, 0:r], hb(S.ident[0:r, 0:r], r, r), LM[0:r, m % 2, :, 0:r],
                                  ALU.subtract).then_inc(ut_ok, 1)
            for q, (lv, m) in enumerate(items):
                r = ROWS[m]
                dve.wait_ge(uy_mm, q + 1)
                dve.tensor_tensor(U[0:r, m, :, 0:r], U[0:r, m, :, 0:r], pb[2 + q % 2][0:r, :, 0:r], ALU.subtract)
                dve.tensor_tensor(T[0:r, m, :, 0:r], T[0:r, m, :, 0:r], pb[4 + q % 2][0:r, :, 0:r], ALU.subtract)\
                    .then_inc(ut_ok, 1)
            for n, m in enumerate(scan):
                r = ROWS[m]
                for h in range(GH):
                    dve.wait_ge(ks_mm, n + 1)
                    if n >= 2 and h == 0:
                        dve.wait_ge(vn_mm, n - 1)
                    dve.scalar_tensor_tensor(out=LM[0:r, n % 2, h, :], in0=pb[0][0:r, h, :],
                                             scalar=v["nbe"][0:r, m, h:h + 1], in1=vb[0:r, m, h, :],
                                             op0=ALU.mult, op1=ALU.add).then_inc(r_ok, 1)
                step(dve.tensor_tensor(T[0:r, m, :, :], pb[1][0:r, :, :], bc(v["egc"][0:r, m, :], r, P), ALU.mult))
                if m < SM:
                    dve.wait_ge(ds_mm, n + 1)
                    for h in range(GH):
                        dve.scalar_tensor_tensor(out=st[:, h, :], in0=st[:, h, :], scalar=gl[:, m, h:h + 1],
                                                 in1=pb[4][:, h, :], op0=ALU.mult, op1=ALU.add)\
                            .then_inc(st_ok, 1)
                else:
                    for q in range(2 * GH):
                        h, half = q // 2, q % 2
                        dve.wait_ge(sds_mm, q + 1)
                        for i in range(4):
                            b = 4 * half + i
                            last = dve.scalar_tensor_tensor(
                                out=s0[:, b, h, :], in0=s0[:, b, h, :], scalar=glS[:, b * GH + h:b * GH + h + 1],
                                in1=pb[4 + q % 2][:, i, :], op0=ALU.mult, op1=ALU.add)
                        last.then_inc(sst_ok, 1)
                    dve.wait_ge(ds_mm, TILES)
                step(dve.tensor_tensor(T[0:r, m, :, :], T[0:r, m, :, :], pb[3][0:r, :, :], ALU.add))
                dve.tensor_tensor(T[0:r, m, :, :], T[0:r, m, :, :], bc(v["rq"][0:r, m, :], r, P), ALU.mult)\
                    .then_inc(o_ok, 1)
            dve.wait_ge(ss_ok, GH * TILES)
            dve.tensor_scalar(v["ss"][:, :, :], v["ss"][:, :, :], 1.0 / P, EPS, ALU.mult, ALU.add).then_inc(yq_ok, 1)
            dve.wait_ge(rst_ok, 1)
            step(dve.reciprocal(v["rst"][:, :, :], v["rst"][:, :, :]))
            for m in range(TILES):
                r = ROWS[m]
                dve.wait_ge(zg_ok, m + 1)
                for h in range(GH):
                    last = dve.scalar_tensor_tensor(out=T[0:r, m, h, :], in0=T[0:r, m, h, :],
                                                    scalar=v["rst"][0:r, m, h:h + 1],
                                                    in1=S.zs[0:r, m, h * P:(h + 1) * P], op0=ALU.mult,
                                                    op1=ALU.mult)
                last.then_inc(og_ok, 1)

        @block.scalar
        def _(act):
            act.wait_ge(nrm_e, 1)
            act.activation(rinv[:, :, :], rinv[:, :, :], ACT.Sqrt).then_inc(root_ok, 1)
            act.wait_ge(gates_in, 1)
            act.activation(v["eb"][:, :, :], gb[:, :, 0:4], ACT.Exp, scale=-1.0).then_inc(exp_ok, 1)
            act.activation(ea[:, :], alog[:, :], ACT.Exp).then_inc(exp_ok, 1)
            act.activation(v["ex"][:, :, :], v["ax"][:, :, :], ACT.Exp).then_inc(exp_ok, 1)
            act.wait_ge(exp_ok, 3)
            act.activation(v["spl"][:, :, :], v["ex"][:, :, :], ACT.Ln, bias=1.0).then_inc(exp_ok, 1)
            act.wait_ge(gc_ok, 1)
            act.activation(v["egc"][:, :, :], v["gcum"][:, :, :], ACT.Exp).then_inc(egc_ok, 1)
            act.activation(v["ek"][:, :, :], v["dk"][:, :, :], ACT.Exp).then_inc(egc_ok, 1)
            act.activation(gl[:, :, :], v["glast"][:, 0:NP, :], ACT.Exp).then_inc(egc_ok, 1)
            act.activation(glS[:, :], glS[:, :], ACT.Exp).then_inc(egc_ok, 1)
            for m in range(TILES):
                r = ROWS[m]
                act.wait_ge(knT_mm, m + 1)
                act.activation(knT[:, m, :, 0:r], pb[6][:, :, 0:r], ACT.Copy).then_inc(knT_ok, 1)
                act.wait_ge(diff_ok, m + 1)
                for h in range(GH):
                    act.activation(dm[0:r, m % 2, h, 0:r], dm[0:r, m % 2, h, 0:r], ACT.Exp,
                                   bias=v["gcum"][0:r, m, h:h + 1])
                    last = act.activation(dt_[0:r, m % 2, h, 0:r], dt_[0:r, m % 2, h, 0:r], ACT.Exp,
                                          bias=v["ngc"][0:r, m, h:h + 1])
                last.then_inc(dec_ok, 1)
            for q, (lv, m) in enumerate(items):
                r = ROWS[m]
                act.wait_ge(y_mm, q + 1)
                if q >= 2:
                    act.wait_ge(uy_mm, q - 1)
                act.activation(Y[0:r, q % 2, :, 0:r], pb[q % 2][0:r, :, 0:r], ACT.Copy).then_inc(y_sb, 1)
            for n, m in enumerate(scan):
                r = ROWS[m]
                act.wait_ge(vn_mm, n + 1)
                if n >= 2:
                    act.wait_ge(ds_mm, n - 1)
                act.activation(Y[0:r, n % 2, :, :], pb[2][0:r, :, :], ACT.Copy).then_inc(vn_sb, 1)
                act.wait_ge(o_ok, n + 1)
                for h in range(GH):
                    if n or h:
                        act.wait_ge(ss_ok, GH * n + h)
                    act.activation(LMJ[0:r, :], T[0:r, m, h, :], ACT.Square,
                                   accum_out=v["ss"][0:r, m, h:h + 1]).then_inc(ss_ok, 1)
            act.wait_ge(yq_ok, 1)
            act.activation(v["rst"][:, :, :], v["ss"][:, :, :], ACT.Sqrt).then_inc(rst_ok, 1)
            for m in range(TILES):
                r = ROWS[m]
                act.wait_ge(ogT_mm, m + 1)
                act.activation(S.mixT[:, 0:GH, m * P:m * P + r], pb[m % 2][:, :, 0:r], ACT.Copy).then_inc(og_out, 1)

        @block.gpsimd
        def _(pool):
            pool.memset(st[:, :, :], 0.0).then_inc(x_ok, 1)
            pool.memset(kx[:, :, :, :], 0.0).then_inc(x_ok, 1)
            pool.memset(qx[:, :, :, :], 0.0).then_inc(x_ok, 1)
            pool.wait_ge(small_in, 48)
            for m in range(TILES):
                r = ROWS[m]
                z = S.zs[0:r, m, :].rearrange("p (h n) -> p h n", h=GH)
                pool.tensor_tensor(z, z, hb(gn[0:r, :], r, P), ALU.mult).then_inc(zg_ok, 1)
            pool.wait_ge(fac_ok, 1)
            for m in range(TILES):
                r = ROWS[m]
                pool.wait_ge(l_ok, 2 * (m + 1))
                pool.tensor_tensor(L[0:r, m, :, 0:r], L[0:r, m, :, 0:r], bc(v["beta"][0:r, m, :], r, r), ALU.mult)\
                    .then_inc(lb_ok, 1)
            for m in range(TILES):
                r = ROWS[m]
                pool.wait_ge(lb_ok, m + 1)
                if m >= 2:
                    pool.wait_ge(ut_ok, m - 1)
                    pool.wait_ge(lt_mm, m - 1)
                pool.tensor_tensor(LM[0:r, m % 2, :, 0:r], L[0:r, m, :, 0:r], hb(S.join[0:r, 0, 0:r], r, r), ALU.mult)\
                    .then_inc(lm_ok, 1)
            for q, (lv, m) in enumerate(items):
                r = ROWS[m]
                n = TILES + q
                if q >= 2:
                    pool.wait_ge(y_mm, q - 1)
                else:
                    pool.wait_ge(ut_ok, TILES)
                    pool.wait_ge(lt_mm, TILES)
                pool.tensor_tensor(LM[0:r, q % 2, :, 0:r], L[0:r, m, :, 0:r], hb(S.join[0:r, lv, 0:r], r, r), ALU.mult)\
                    .then_inc(lm_ok, 1)
            pool.wait_ge(lm_ok, TILES + len(items))
            for m in range(TILES):
                r = ROWS[m]
                pool.tensor_tensor(L[0:r, m, :, :], kn[0:r, m, :, :], bc(v["ek"][0:r, m, :], r, P), ALU.mult)\
                    .then_inc(kd_ok, 1)
            pool.wait_ge(x_ok, 3)
            for b in range(DEC_BATCH):
                c = slice(b * DEC_SEQ, (b + 1) * DEC_SEQ)
                pool.tensor_copy(kx[:, :, b, c], knT[:, SM, :, c])
                last = pool.tensor_copy(qx[:, :, b, c], S.cs[:, 0:GH, SEQ + b * DEC_SEQ:SEQ + (b + 1) * DEC_SEQ])
            last.then_inc(x_ok, 1)
            pool.wait_ge(kd_ok, TILES)
            for h in range(GH):
                buf = (dm, dt_)[h % 2]
                if h >= 2:
                    pool.wait_ge(sds_mm, 2 * (h - 1))
                for b in range(DEC_BATCH):
                    last = pool.tensor_scalar(kdx(buf)[:, b, :], L[0:NSAMP, SM, h, :], S.seq_pick[:, b:b + 1], None,
                                              ALU.mult)
                last.then_inc(kdx_ok, 1)

        @block.tensor
        def _(pe):
            pe.wait_ge(g_ok, 1)
            sums = pb[5][:, 0, 0:TILES * 8].rearrange("p (m e) -> p m e", e=8)
            for m in range(TILES):
                r = ROWS[m]
                up, on = (S.upper, S.ones) if m < SM else (S.seq_upper, S.seq_ones)
                pe.matmul(sums[0:r, m, 0:4], up[0:r, 0:r], v["g"][0:r, m, :], start=True, stop=True)
                pe.matmul(sums[0:r, m, 4:8], on[0:r, 0:r], v["g"][0:r, m, :], start=True, stop=True)
            pe.matmul(pb[5][:, 1, 0:DEC_BATCH * GH], S.ones[0:NSAMP, :], gsel[:, :, :].rearrange("p b h -> p (b h)"),
                      start=True, stop=True).then_inc(gc_mm, 1)
            pe.wait_ge(fac_ok, 1)
            for m in range(TILES):
                r = ROWS[m]
                t = slice(m * P, m * P + r)
                if m >= 1:
                    pe.wait_ge(kn_ok, m)
                    pe.wait_ge(vb_ok, m)
                for h in range(GH):
                    pe.transpose(pb[0][0:r, h, :], S.cs[:, GH + h, t], S.ident[:, :])
                for h in range(GH):
                    mm = pe.transpose(pb[1][0:r, h, :], S.cs[:, 2 * GH + h, t], S.ident[:, :])
                mm.then_inc(kT_mm, 1)
                if m >= 1:
                    pe.wait_ge(diff_ok, m)
                up = S.upper if m < SM else S.seq_upper
                for h in range(GH):
                    mm = pe.matmul(pb[2][0:r, h, 0:r], v["g"][0:r, m, h:h + 1].to_broadcast([r, r]), up[0:r, 0:r],
                                   start=True, stop=True)
                mm.then_inc(gr_mm, 1)
                pe.wait_ge(kn_ok, m + 1)
                if m >= 1:
                    pe.wait_ge(knT_ok, m)
                for h in range(GH):
                    mm = pe.transpose(pb[6][:, h, 0:r], kn[0:r, m, h, :], S.ident[0:r, 0:r])
                mm.then_inc(knT_mm, 1)
                pe.wait_ge(knT_ok, m + 1)
                if m >= 1:
                    pe.wait_ge(l_ok, 2 * m)
                for h in range(GH):
                    pe.matmul(pb[3][0:r, h, 0:r], knT[:, m, h, 0:r], knT[:, m, h, 0:r], start=True, stop=True)
                for h in range(GH):
                    mm = pe.matmul(pb[4][0:r, h, 0:r], knT[:, m, h, 0:r], S.cs[:, h, t], start=True, stop=True)
                mm.then_inc(kk_mm, 1)
            for m in range(TILES):
                r = ROWS[m]
                pe.wait_ge(lm_ok, m + 1)
                if m == 0:
                    pe.wait_ge(vb_ok, TILES)
                if m >= 2:
                    pe.wait_ge(ut_ok, m - 1)
                for h in range(GH):
                    mm = pe.transpose(pb[m % 2][0:r, h, 0:r], LM[0:r, m % 2, h, 0:r], S.ident[0:r, 0:r])
                mm.then_inc(lt_mm, 1)

            def y_product(q):
                lv, m = items[q]
                r = ROWS[m]
                pe.wait_ge(lm_ok, TILES + q + 1)
                pe.wait_ge(ut_ok, TILES if before[q] is None else TILES + before[q] + 1)
                if q >= 2:
                    pe.wait_ge(y_sb, q - 1)
                for h in range(GH):
                    mm = pe.matmul(pb[q % 2][0:r, h, 0:r], LM[0:r, q % 2, h, 0:r], U[0:r, m, h, 0:r],
                                   start=True, stop=True)
                mm.then_inc(y_mm, 1)

            y_product(0)
            for q, (lv, m) in enumerate(items):
                r = ROWS[m]
                if q + 1 < len(items):
                    y_product(q + 1)
                pe.wait_ge(y_sb, q + 1)
                if q >= 2:
                    pe.wait_ge(ut_ok, TILES + q - 1)
                for h in range(GH):
                    pe.matmul(pb[2 + q % 2][0:r, h, 0:r], T[0:r, m, h, 0:r], Y[0:r, q % 2, h, 0:r],
                              start=True, stop=True)
                for h in range(GH):
                    mm = pe.matmul(pb[4 + q % 2][0:r, h, 0:r], Y[0:r, q % 2, h, 0:r], T[0:r, m, h, 0:r],
                                   start=True, stop=True)
                mm.then_inc(uy_mm, 1)
            pe.wait_ge(ut_ok, TILES + len(items))
            pe.wait_ge(x_ok, 4)
            pe.wait_ge(kd_ok, TILES)
            pe.wait_ge(s0_in, 16)
            for n, m in enumerate(scan):
                r = ROWS[m]
                t = slice(m * P, m * P + r)
                if n >= 1:
                    pe.wait_ge(r_ok, GH * n)
                    pe.wait_ge(o_ok, n)
                if m < SM:
                    for h in range(GH):
                        if n >= 1:
                            pe.wait_ge(st_ok, GH * (n - 1) + h + 1)
                        pe.matmul(pb[0][0:r, h, :], knT[:, m, h, 0:r], st[:, h, :], start=True, stop=True)
                    for h in range(GH):
                        mm = pe.matmul(pb[1][0:r, h, :], S.cs[:, h, t], st[:, h, :], start=True, stop=True)
                else:
                    for h in range(GH):
                        for b in range(DEC_BATCH):
                            pe.matmul(pb[0][0:r, h, :], kx[:, h, b, :], s0[:, b, h, :], start=(b == 0),
                                      stop=(b == DEC_BATCH - 1))
                        for b in range(DEC_BATCH):
                            mm = pe.matmul(pb[1][0:r, h, :], qx[:, h, b, :], s0[:, b, h, :], start=(b == 0),
                                           stop=(b == DEC_BATCH - 1))
                mm.then_inc(ks_mm, 1)
                if n >= 1:
                    pe.wait_ge(vn_sb, n)
                for h in range(GH):
                    pe.wait_ge(r_ok, GH * n + h + 1)
                    mm = pe.matmul(pb[2][0:r, h, :], U[0:r, m, h, 0:r], LM[0:r, n % 2, h, :], start=True, stop=True)
                mm.then_inc(vn_mm, 1)
                pe.wait_ge(vn_sb, n + 1)
                for h in range(GH):
                    vn = Y[0:r, n % 2, h, :]
                    mm = pe.matmul(pb[3][0:r, h, :], aT[0:r, m, h, 0:r], vn, start=True, stop=True)
                    if m < SM:
                        mm = pe.matmul(pb[4][:, h, :], L[0:r, m, h, :], vn, start=True, stop=True)
                mm.then_inc(ds_mm, 1)
            for q in range(2 * GH):
                h, half = q // 2, q % 2
                pe.wait_ge(kdx_ok, h + 1)
                if q >= 2:
                    pe.wait_ge(sst_ok, q - 1)
                for i in range(4):
                    mm = pe.matmul(pb[4 + q % 2][:, i, :], kdx((dm, dt_)[h % 2])[:, 4 * half + i, :],
                                   Y[0:NSAMP, NP % 2, h, :], start=True, stop=True)
                mm.then_inc(sds_mm, 1)
            for m in range(TILES):
                r = ROWS[m]
                pe.wait_ge(og_ok, m + 1)
                if m >= 2:
                    pe.wait_ge(og_out, m - 1)
                for h in range(GH):
                    mm = pe.transpose(pb[m % 2][:, h, 0:r], T[0:r, m, h, :], S.ident[0:r, 0:r])
                mm.then_inc(ogT_mm, 1)


NH = 8
HD = 64
GROUPS = 2
PH = NH // GROUPS
NB = SEQ // 32
REL_BUCKETS = 32
PAST = 1024
D_MAX = PAST + DEC_SEQ - 1
TABLE = D_MAX + P
WIN = 512
WTABLE = WIN + DEC_SEQ - 1
SCALE = HD ** -0.5
NK = PAST // P
CB = PAST // 32
FLOOR = -1e29


def bucket_starts():
    d = np.arange(D_MAX + 1)
    exact = REL_BUCKETS // 2
    df = np.maximum(d, 1).astype(np.float32)
    far = exact + (np.log(df / np.float32(exact)) / np.float32(math.log(2048 / exact))
                   * np.float32(REL_BUCKETS - exact)).astype(np.int32)
    b = np.where(d < exact, d, np.minimum(far, REL_BUCKETS - 1))
    return [int(x) for x in np.searchsorted(b, np.arange(b[-1] + 2))]


def keys_stage(nc, I, O, S, scratch):
    NG = 18
    W = NG * HD
    with ExitStack() as ctx:
        a = scope(nc, ctx, "ky")
        gq, gk = a.sb("gq", [P, HD]), a.sb("gk", [P, 3, HD])
        gain = a.sb("gain", [P, NG, HD])
        sq = a.sb("sq", [P, 2, NG, HD])
        qp = a.sb("qp", [P, 2, PH, GROUPS, HD])
        rs = a.sb("rs", [P, TILES, NG])
        relT = a.sb("relT", [NH, REL_BUCKETS])
        back = a.sb("back", [P, NH, SEQ])
        turn = a.sb("turn", [P, P])
        pb = [a.ps(f"pb{i}", [P, SEQ]) for i in range(2)]
        back_in, turn_ok, back_mm, back_a, back_v = (a.sem(n) for n in (
            "back_in", "turn_ok", "back_mm", "back_a", "back_v"))
        tab = a.sb("tab", [NH, TABLE])
        tabw = a.sb("tabw", [NH, WTABLE])
        pT = [a.ps(f"pT{i}", [P, 4, P]) for i in range(2)]
        pk = [a.ps(f"pk{i}", [P, 4, P]) for i in range(2)]
        pc = a.ps("pc", [P, NB])
        pv = a.ps("pv", [P, P])
        gains_in, rel_in, gain_ok, sq_ok, ss_ok, rs_ok, root_ok, hg_ok, hn_ok = (a.sem(n) for n in (
            "gains_in", "rel_in", "gain_ok", "sq_ok", "ss_ok", "rs_ok", "root_ok", "hg_ok", "hn_ok"))
        tab_ok, tab_out, bias_in, stored, gex_ok = (a.sem(n) for n in (
            "tab_ok", "tab_out", "bias_in", "stored", "gex_ok"))
        qT_mm, kT_mm, qT_ok, kT_ok, cmp_mm, qbd_ok, gate_ok, gate_out = (a.sem(n) for n in (
            "qT_mm", "kT_mm", "qT_ok", "kT_ok", "cmp_mm", "qbd_ok", "gate_ok", "gate_out"))
        chain, ac_chain = a.sem("chain"), a.sem("ac_chain")
        block = ctx.enter_context(nc.Block())
        starts = bucket_starts()

        def dram(t, offset, dims):
            return bass.AP(t.tensor, offset, dims)

        @block.sync
        def _(sp):
            sp.dma_start(gq[:, :], I["nsa_q_norm"].to_broadcast([P, HD])).then_inc(gains_in, 16)
            sp.dma_start(gk[:, :, :], I["nsa_k_norm"].to_broadcast([P, 3, HD])).then_inc(gains_in, 16)
            sp.dma_start(relT[:, :], I["rel_bias"].rearrange("b h -> h b"),
                         allow_slow_non_contiguous=True).then_inc(rel_in, 16)
            sp.dma_start(O["win_sample"][0, :, 0:WIN - DEC_SEQ], I["state_win_kv"][0, :, DEC_SEQ:WIN])\
                .then_inc(stored, 16)
            sp.wait_ge(tab_ok, 1)
            for b in range(4):
                sp.dma_start(scratch["tab"][b], tab[:, :]).then_inc(tab_out, 16)
                sp.dma_start(scratch["tabw"][b], tabw[:, :]).then_inc(tab_out, 16)
            sp.wait_ge(tab_out, 16 * 8)
            sp.dma_start(back[:, :, :], dram(scratch["tab"], D_MAX - (SEQ - P) - (P - 1), [[1, P], [TABLE, NH], [1, SEQ]]))\
                .then_inc(back_in, 16)
            for t in range(DEC_SEQ):
                sp.dma_start(S.bias_s[t:P:DEC_SEQ, 0:PAST + DEC_SEQ],
                             dram(scratch["tab"], DEC_SEQ - 1 - t, [[TABLE, 4 * NH], [1, PAST + DEC_SEQ]]))\
                    .then_inc(bias_in, 16)
                sp.dma_start(S.bias_w[t:P:DEC_SEQ, :],
                             dram(scratch["tabw"], DEC_SEQ - 1 - t, [[WTABLE, 4 * NH], [1, WIN]]))\
                    .then_inc(bias_in, 16)
            for m in range(TILES - 1):
                sp.wait_ge(hn_ok, m + 1)
                rows = slice(m * P, (m + 1) * P)
                sp.dma_start(O["kv_rows_prompt"][0, 0, rows].rearrange("t s g d -> t (s g d)"),
                             S.h_tok[:, m, C_KV:C_WIN]).then_inc(stored, 16)
                sp.dma_start(O["win_prompt"][0, 0, rows].rearrange("t s g d -> t (s g d)"),
                             S.h_tok[:, m, C_WIN:C_G]).then_inc(stored, 16)
            sp.wait_ge(hn_ok, TILES)
            sp.dma_start(O["kv_rows_sample"][0].rearrange("b t s g d -> (b t) (s g d)"),
                         S.h_tok[0:NSAMP, TILES - 1, C_KV:C_WIN]).then_inc(stored, 16)
            for b in range(DEC_BATCH):
                sp.dma_start(O["win_sample"][0, b, WIN - DEC_SEQ:WIN].rearrange("t s g d -> t (s g d)"),
                             S.h_tok[b * DEC_SEQ:(b + 1) * DEC_SEQ, TILES - 1, C_WIN:C_G]).then_inc(stored, 16)
            sp.wait_ge(gate_ok, 1)
            for t in range(DEC_SEQ):
                sp.dma_start(scratch["gates"][t], S.gates[t:NSAMP:DEC_SEQ, TILES - 1, :]).then_inc(gate_out, 16)
            sp.wait_ge(gate_out, 16 * DEC_SEQ)
            for t in range(DEC_SEQ):
                for bb in range(2):
                    sp.dma_start(S.gates_s[t:P:DEC_SEQ, bb, :],
                                 dram(scratch["gates"], (t * DEC_BATCH + 4 * bb) * 24, [[3, 4 * NH], [1, 3]]))\
                        .then_inc(bias_in, 16)
            sp.wait_ge(stored, 16 * (2 * TILES + DEC_BATCH))
            sp.wait_ge(bias_in, 16 * 4 * DEC_SEQ)

        @block.vector
        def _(dve):
            step = Chain(dve, chain)
            dve.wait_ge(gains_in, 32)
            step(dve.memset(gain[:, :, :], 1.0))
            gb = lambda x, n: x.unsqueeze(1).to_broadcast([P, n, HD])
            step(dve.tensor_scalar(gain[:, 0:8, :], gb(gq[:, :], 8), SCALE, None, ALU.mult))
            for i, at in enumerate((8, 12, 16)):
                step(dve.tensor_copy(gain[:, at:at + 2, :], gb(gk[:, i, :], 2)))
            dve.memset(rs[:, :, :], 1.0).then_inc(gain_ok, 1)
            dve.wait_ge(gain_ok, 1)
            for m in range(TILES):
                r = ROWS[m]
                dve.wait_ge(sq_ok, m + 1)
                dve.tensor_reduce(rs[0:r, m, :], sq[0:r, m % 2, :, :], AX.X, ALU.add).then_inc(ss_ok, 1)
            dve.wait_ge(ss_ok, TILES)
            dve.tensor_scalar(rs[:, :, :], rs[:, :, :], 1.0 / HD, EPS, ALU.mult, ALU.add).then_inc(rs_ok, 1)
            dve.wait_ge(rel_in, 16)
            step(dve.memset(tab[:, D_MAX + 1:TABLE], NEG))
            for j in range(len(starts) - 1):
                lo, hi = starts[j], starts[j + 1]
                last = dve.tensor_copy(tab[:, D_MAX + 1 - hi:D_MAX + 1 - lo], relT[:, j:j + 1].to_broadcast([NH, hi - lo]))
            step(last)
            step(dve.tensor_copy(tabw[:, :], tab[:, PAST - WIN:PAST - WIN + WTABLE]))
            dve.memset(tabw[:, 0:DEC_SEQ - 1], NEG).then_inc(tab_ok, 1)
            dve.wait_ge(root_ok, 1)
            step(dve.reciprocal(rs[:, :, :], rs[:, :, :]))
            for g in (10, 14):
                step(dve.memset(rs[:, :, g:g + 2], 1.0))

            def keep_kT(m):
                dve.wait_ge(kT_mm, m + 1)
                dve.tensor_copy(S.kT[:, :, m * P:m * P + ROWS[m]], pk[m % 2][:, 0:2, 0:ROWS[m]]).then_inc(kT_ok, 1)

            for m in range(TILES):
                r = ROWS[m]
                h = S.h_tok[0:r, m, C_NQ:C_NQ + W].rearrange("p (g d) -> p g d", d=HD)
                if m >= 1:
                    keep_kT(m - 1)
                dve.wait_ge(hg_ok, m + 1)
                if m >= 2:
                    dve.wait_ge(qT_mm, m - 1)
                for g in range(GROUPS):
                    c = slice(g * PH, (g + 1) * PH)
                    dve.tensor_tensor(qp[0:r, m % 2, :, g, :], h[:, c, :],
                                      rs[0:r, m, c].unsqueeze(2).to_broadcast([r, PH, HD]), ALU.mult)
                dve.tensor_tensor(h[:, NH:, :], h[:, NH:, :],
                                  rs[0:r, m, NH:].unsqueeze(2).to_broadcast([r, NG - NH, HD]), ALU.mult)\
                    .then_inc(hn_ok, 1)
            keep_kT(TILES - 1)
            dve.wait_ge(gex_ok, 2)
            step(dve.tensor_scalar(S.gates[:, :, :], S.gates[:, :, :], 1.0, None, ALU.add))
            dve.reciprocal(S.gates[:, :, :], S.gates[:, :, :]).then_inc(gate_ok, 1)
            dve.wait_ge(cmp_mm, 1)
            step(dve.memset(S.kcT[:, :, :], 0.0))
            for g in range(GROUPS):
                rows = slice(g * HD, (g + 1) * HD)
                dve.tensor_copy(S.kcT[rows, g, :], pc[rows, :])
            vrep = pv[:, :].rearrange("p (g d) -> p g d", g=GROUPS)
            for g in range(GROUPS):
                for j in range(PH):
                    h = g * PH + j
                    last = dve.tensor_scalar(S.vbd[:, h, :], vrep[:, g, :], S.head_rows[:, h:h + 1], None, ALU.mult)
            step(last)
            dve.wait_ge(qT_ok, TILES)
            dve.wait_ge(qbd_ok, 1)
            for g in range(GROUPS):
                rows = slice(g * HD, (g + 1) * HD)
                last = dve.tensor_copy(S.qbd[rows, :, g, :, :],
                                       S.qT[rows, :, SEQ:TOK].rearrange("p j (b t) -> p b j t", t=DEC_SEQ))
            step(last)
            for h in range(1, NH, 2):
                dve.wait_ge(back_mm, h + 1)
                dve.tensor_copy(S.bias[:, h, :], pb[1][:, :]).then_inc(back_v, 1)

        @block.scalar
        def _(act):
            step = Chain(act, ac_chain)
            for m in range(TILES):
                r = ROWS[m]
                if m >= 2:
                    act.wait_ge(ss_ok, m - 1)
                act.activation(sq[0:r, m % 2, :, :].rearrange("p g d -> p (g d)"), S.h_tok[0:r, m, C_NQ:C_NQ + W],
                               ACT.Square).then_inc(sq_ok, 1)
            act.wait_ge(rs_ok, 1)
            act.activation(rs[:, :, :], rs[:, :, :], ACT.Sqrt).then_inc(root_ok, 1)
            act.wait_ge(qbd_ok, 2)
            act.activation(S.gates[:, 0:TILES - 1, :], S.h_tok[:, 0:TILES - 1, C_G:COLS], ACT.Exp, scale=-1.0)\
                .then_inc(gex_ok, 1)
            act.activation(S.gates[0:NSAMP, TILES - 1, :], S.h_tok[0:NSAMP, TILES - 1, C_G:COLS], ACT.Exp, scale=-1.0)\
                .then_inc(gex_ok, 1)
            for m in range(TILES):
                r = ROWS[m]
                act.wait_ge(qT_mm, m + 1)
                act.activation(S.qT[:, :, m * P:m * P + r], pT[m % 2][:, :, 0:r], ACT.Copy).then_inc(qT_ok, 1)
            for h in range(0, NH, 2):
                act.wait_ge(back_mm, h + 1)
                act.activation(S.bias[:, h, :], pb[0][:, :], ACT.Copy).then_inc(back_a, 1)

        @block.gpsimd
        def _(pool):
            pool.memset(S.qbd[:, :, :, :, :], 0.0).then_inc(qbd_ok, 1)
            pool.memset(S.gates[:, :, :], 0.0).then_inc(qbd_ok, 1)
            pool.memset(turn[:, :], 0.0).then_inc(turn_ok, 1)
            pool.wait_ge(turn_ok, 1)
            pool.affine_select(out=turn[:, :], in_=turn[:, :], compare_op=ALU.not_equal, fill=1.0,
                               base=1 - P, pattern=[[1, P]], channel_multiplier=1).then_inc(turn_ok, 1)
            pool.wait_ge(gain_ok, 1)
            pool.wait_ge(sq_ok, TILES)
            for m in range(TILES):
                r = ROWS[m]
                h = S.h_tok[0:r, m, C_NQ:C_NQ + W].rearrange("p (g d) -> p g d", d=HD)
                pool.tensor_tensor(h, h, gain[0:r, :, :], ALU.mult).then_inc(hg_ok, 1)

        @block.tensor
        def _(pe):
            for m in range(TILES):
                r = ROWS[m]
                pe.wait_ge(hn_ok, m + 1)
                if m >= 2:
                    pe.wait_ge(qT_ok, m - 1)
                    pe.wait_ge(kT_ok, m - 1)
                for j in range(PH):
                    mm = pe.transpose(pT[m % 2][:, j, 0:r], qp[0:r, m % 2, j, :, :].rearrange("p g d -> p (g d)"),
                                      S.ident[0:r, 0:r])
                mm.then_inc(qT_mm, 1)
                for i, c in enumerate((C_KV + 256, C_WIN)):
                    mm = pe.transpose(pk[m % 2][:, i, 0:r], S.h_tok[0:r, m, c:c + P], S.ident[0:r, 0:r])
                mm.then_inc(kT_mm, 1)
            for m in range(TILES - 1):
                pe.matmul(pc[:, 4 * m:4 * m + 4], S.h_tok[:, m, C_KV:C_KV + P], S.mean[:, CB - 4:CB],
                          start=True, stop=True)
                mm = pe.matmul(pv[:, :], S.mean_rep[:, m, :], S.h_tok[:, m, C_KV + P:C_KV + 2 * P],
                               start=(m == 0), stop=(m == TILES - 2))
            mm.then_inc(cmp_mm, 1)
            pe.wait_ge(turn_ok, 2)
            pe.wait_ge(back_in, 16)
            for h in range(NH):
                if h >= 2:
                    pe.wait_ge(back_v if h % 2 else back_a, h // 2)
                pe.matmul(pb[h % 2][:, :], turn[:, :], back[:, h, :], start=True, stop=True).then_inc(back_mm, 1)


def attend_prompt_stage(nc, I, O, S):
    NQ = TILES - 1
    with ExitStack() as ctx:
        a = scope(nc, ctx, "ap")
        lg = a.sb("lg", [P, 2, 2, SEQ])
        pt = a.sb("pt", [P, 2, 2, 4, P])
        lc = a.sb("lc", [P, NH, NB])
        pct = a.sb("pct", [P, P])
        mx, nm = a.sb("mx", [P, NQ, NH, 2]), a.sb("nm", [P, NQ, NH, 2])
        sm = a.sb("sm", [P, NQ, 3, NH])
        cf = a.sb("cf", [P, NQ, 3, NH])
        mc = a.sb("mc", [P, NH])
        oc = a.sb("oc", [P, 3, NH, HD])
        p_s = [a.ps(f"p_s{i}", [P, SEQ]) for i in range(2)]
        p_t = [a.ps(f"p_t{i}", [P, 4, P]) for i in range(2)]
        p_o = [a.ps(f"p_o{i}", [P, NH, HD]) for i in range(3)]
        p_c = a.ps("p_c", [P, 4, P])
        s_mm, lg_ok, nm_ok, e_ok, t_mm, t_ok, pv_mm = (a.sem(n) for n in (
            "s_mm", "lg_ok", "nm_ok", "e_ok", "t_mm", "t_ok", "pv_mm"))
        c_mm, c_lg, c_e, c_ok, ct_mm, ct_ok, cpv_mm, o_ok, oT_mm, oT_ok, z_ok = (a.sem(n) for n in (
            "c_mm", "c_lg", "c_e", "c_ok", "ct_mm", "ct_ok", "cpv_mm", "o_ok", "oT_mm", "oT_ok", "z_ok"))
        chain = a.sem("chain")
        items = [(qt, h) for qt in range(NQ) for h in range(NH)]
        V_COL = (C_KV + 3 * P, C_WIN + P)
        block = ctx.enter_context(nc.Block())

        @block.tensor
        def _(pe):
            def scores(i):
                qt, h = items[i]
                g, j = h // PH, h % PH
                rows, nk = slice(g * HD, (g + 1) * HD), (qt + 1) * P
                for br in range(2):
                    if i >= 1:
                        pe.wait_ge(lg_ok, 2 * (i - 1) + br + 1)
                    pe.matmul(p_s[br][:, 0:nk], S.qT[rows, j, qt * P:(qt + 1) * P], S.kT[rows, br, 0:nk],
                              start=True, stop=True).then_inc(s_mm, 1)

            def turn(i):
                qt, h = items[i]
                for br in range(2):
                    pe.wait_ge(e_ok, 2 * i + br + 1)
                    if i >= 1:
                        pe.wait_ge(t_ok, 2 * (i - 1) + br + 1)
                    for kt in range(qt + 1):
                        mm = pe.transpose(p_t[br][:, kt, :], lg[:, i % 2, br, kt * P:(kt + 1) * P], S.ident[:, :])
                    mm.then_inc(t_mm, 1)

            def values(i):
                qt, h = items[i]
                g = h // PH
                if h == 0 and qt >= 1:
                    pe.wait_ge(o_ok, qt)
                for br in range(2):
                    pe.wait_ge(t_ok, 2 * i + br + 1)
                    for kt in range(qt + 1):
                        c = V_COL[br] + g * HD
                        mm = pe.matmul(p_o[br][:, h, :], pt[:, i % 2, br, kt, :], S.h_tok[:, kt, c:c + HD],
                                       start=(kt == 0), stop=(kt == qt))
                mm.then_inc(pv_mm, 1)

            def compressed(qt):
                nb = 4 * (qt + 1)
                if qt >= 1:
                    pe.wait_ge(oT_ok, qt)
                sc = p_c[:, 0, :].rearrange("p (g j n) -> p g j n", g=GROUPS, j=PH)
                for j in range(PH):
                    mm = pe.matmul(sc[:, :, j, 0:nb], S.qT[:, j, qt * P:(qt + 1) * P], S.kcT[:, :, 0:nb],
                                   start=True, stop=True)
                mm.then_inc(c_mm, 1)
                pe.wait_ge(c_ok, qt + 1)
                pe.transpose(p_c[:, 1, :], lc[:, :, :].rearrange("p h n -> p (h n)"), S.ident[:, :]).then_inc(ct_mm, 1)
                pe.wait_ge(ct_ok, qt + 1)
                pe.matmul(p_o[2][:, :, :].rearrange("p h d -> p (h d)"), pct[:, :],
                          S.vbd[:, :, :].rearrange("p h d -> p (h d)"), start=True, stop=True).then_inc(cpv_mm, 1)

            def to_mix(qt):
                pe.wait_ge(o_ok, qt + 1)
                o = oc[:, 0, :, :].rearrange("p h d -> p (h d)")
                for j in range(4):
                    mm = pe.transpose(p_c[:, j, :], o[:, j * P:(j + 1) * P], S.ident[:, :])
                mm.then_inc(oT_mm, 1)

            n = len(items)
            for i in range(n + 2):
                if i >= 2 and items[i - 2][1] == NH - 1:
                    values(i - 2)
                    compressed_at = items[i - 2][0]
                    to_mix(compressed_at)
                    if i < n:
                        compressed(items[i][0])
                elif i >= 2:
                    values(i - 2)
                if i == 0:
                    compressed(0)
                if i < n:
                    scores(i)
                if 1 <= i <= n:
                    turn(i - 1)

        @block.vector
        def _(dve):
            step = Chain(dve, chain)
            dve.memset(lc[:, :, :], 0.0).then_inc(z_ok, 1)
            dve.wait_ge(z_ok, 1)

            def compressed(qt):
                nb = 4 * (qt + 1)
                dve.wait_ge(c_mm, qt + 1)
                sc = p_c[:, 0, :].rearrange("p (h n) -> p h n", h=NH)[:, :, 0:nb]
                y0 = SEQ - P - qt * P + 31
                l = lc[:, :, 0:nb]
                step(dve.tensor_tensor(l, sc, S.bias[:, :, y0:y0 + 32 * (nb - 1) + 1:32], ALU.add))
                step(dve.tensor_reduce(mc[:, :], l, AX.X, ALU.max))
                step(dve.tensor_scalar(mc[:, :], mc[:, :], FLOOR, None, ALU.max))
                dve.tensor_tensor(l, l, mc[:, :].unsqueeze(2).to_broadcast([P, NH, nb]), ALU.subtract).then_inc(c_lg, 1)
                dve.wait_ge(c_e, qt + 1)
                dve.tensor_reduce(sm[:, qt, 2, :], l, AX.X, ALU.add).then_inc(c_ok, 1)

            def logits(i):
                qt, h = items[i]
                nk = (qt + 1) * P
                for br in range(2):
                    dve.wait_ge(s_mm, 2 * i + br + 1)
                    if i >= 2:
                        dve.wait_ge(t_mm, 2 * (i - 2) + br + 1)
                    dve.tensor_tensor_reduce(lg[:, i % 2, br, 0:nk], p_s[br][:, 0:nk], S.bias[:, h, SEQ - nk:SEQ],
                                             1.0, FLOOR, ALU.add, ALU.max, mx[:, qt, h, br:br + 1]).then_inc(lg_ok, 1)
                dve.wait_ge(lg_ok, 2 * i + 2)
                dve.tensor_scalar(nm[:, qt, h, :], mx[:, qt, h, :], -1.0, None, ALU.mult).then_inc(nm_ok, 1)

            def copy_turned(i):
                qt, h = items[i]
                dve.wait_ge(t_mm, 2 * i + 2)
                if i >= 2:
                    dve.wait_ge(pv_mm, i - 1)
                dve.wait_ge(t_ok, 2 * i + 1)
                dve.tensor_copy(pt[:, i % 2, 1, 0:qt + 1, :], p_t[1][:, 0:qt + 1, :]).then_inc(t_ok, 1)

            def combine(qt):
                dve.wait_ge(pv_mm, NH * (qt + 1))
                dve.wait_ge(cpv_mm, qt + 1)
                dve.wait_ge(e_ok, 2 * NH * (qt + 1))
                step(dve.tensor_scalar(cf[:, qt, :, :], sm[:, qt, :, :], 1e-30, None, ALU.max))
                step(dve.reciprocal(cf[:, qt, :, :], cf[:, qt, :, :]))
                gt = S.gates[:, qt, :].rearrange("p (h b) -> p b h", b=3)
                step(dve.tensor_tensor(cf[:, qt, 0:2, :], cf[:, qt, 0:2, :], gt[:, 1:3, :], ALU.mult))
                step(dve.tensor_tensor(cf[:, qt, 2, :], cf[:, qt, 2, :], gt[:, 0, :], ALU.mult))
                if qt >= 1:
                    dve.wait_ge(oT_mm, qt)
                for br in range(3):
                    last = dve.tensor_tensor(oc[:, br, :, :], p_o[br][:, :, :],
                                             cf[:, qt, br, :].unsqueeze(2).to_broadcast([P, NH, HD]), ALU.mult)
                step(last)
                step(dve.tensor_tensor(oc[:, 0, :, :], oc[:, 0, :, :], oc[:, 1, :, :], ALU.add))
                dve.tensor_tensor(oc[:, 0, :, :], oc[:, 0, :, :], oc[:, 2, :, :], ALU.add).then_inc(o_ok, 1)

            n = len(items)
            compressed(0)
            for i in range(n + 2):
                if i >= 2 and items[i - 2][1] == NH - 1:
                    combine(items[i - 2][0])
                    if i < n:
                        compressed(items[i][0])
                if i < n:
                    logits(i)
                if 1 <= i <= n:
                    copy_turned(i - 1)

        @block.scalar
        def _(act):
            def compressed(qt):
                nb = 4 * (qt + 1)
                l = lc[:, :, 0:nb]
                act.wait_ge(c_lg, qt + 1)
                act.activation(l, l, ACT.Exp).then_inc(c_e, 1)
                act.wait_ge(ct_mm, qt + 1)
                act.activation(pct[:, :], p_c[:, 1, :], ACT.Copy).then_inc(ct_ok, 1)

            def exps(i):
                qt, h = items[i]
                nk = (qt + 1) * P
                act.wait_ge(nm_ok, i + 1)
                for br in range(2):
                    act.activation(lg[:, i % 2, br, 0:nk], lg[:, i % 2, br, 0:nk], ACT.Exp,
                                   bias=nm[:, qt, h, br:br + 1], accum_out=sm[:, qt, br, h:h + 1]).then_inc(e_ok, 1)

            def copy_turned(i):
                qt, h = items[i]
                act.wait_ge(t_mm, 2 * i + 1)
                if i >= 1:
                    act.wait_ge(t_ok, 2 * i)
                if i >= 2:
                    act.wait_ge(pv_mm, i - 1)
                act.activation(pt[:, i % 2, 0, 0:qt + 1, :], p_t[0][:, 0:qt + 1, :], ACT.Copy).then_inc(t_ok, 1)

            def to_mix(qt):
                act.wait_ge(oT_mm, qt + 1)
                act.activation(S.mixT[:, GH:KD, qt * P:(qt + 1) * P], p_c[:, :, :], ACT.Copy).then_inc(oT_ok, 1)

            n = len(items)
            compressed(0)
            for i in range(n + 2):
                if i >= 2 and items[i - 2][1] == NH - 1:
                    to_mix(items[i - 2][0])
                    if i < n:
                        compressed(items[i][0])
                if i < n:
                    exps(i)
                if 1 <= i <= n:
                    copy_turned(i - 1)


def attend_sample_stage(nc, I, O, S):
    PAGES = PAST // P
    NEW = NSAMP
    NQB = 4
    VS, VC = 3 * P, P
    A_USES, D_USES = 2 * NQB + 3, 2 * NQB + 2
    LO, HI = 1, 15
    with ExitStack() as ctx:
        a = scope(nc, ctx, "as")
        pages = a.sb("pages", [P, NQB, PAGES, 4 * P])
        win = S.conv_in[:, :, :].rearrange("p c w -> p (c w)")[:, 0:NQB * 4 * 2 * P]\
            .rearrange("p (b k c) -> p b k c", b=NQB, k=4)
        over = S.bias[:, :, :].rearrange("p h k -> p (h k)")
        kT = over[:, 0:2 * PAST].rearrange("p (two k) -> p two k", two=2)
        kwT = over[:, 2 * PAST:2 * PAST + 2 * WIN].rearrange("p (two k) -> p two k", two=2)
        pts = over[:, 2 * PAST + 2 * WIN:2 * PAST + 2 * WIN + PAST].rearrange("p (n k) -> p n k", k=P)
        kc = a.sb("kc", [P, 2, CB])
        vc = a.sb("vc", [CB, NQB, P])
        under = S.qT[:, :, :].rearrange("p j t -> p (j t)")
        ls = under[:, 0:PAST + NEW]
        lw = under[:, PAST + NEW:PAST + WIN + 2 * NEW]
        lc = a.sb("lc", [P, CB])
        nb = a.sb("nb", [P, 2, DEC_BATCH, DEC_SEQ])
        ptw = a.sb("ptw", [P, 4, P])
        ptn = a.sb("ptn", [NEW, 3, P])
        table = a.sb("table", [P, DEC_BATCH * PAGES], I32)
        row, rowf = a.sb("row", [P, 1], I32), a.sb("rowf", [P, 1])
        idx = a.sb("idx", [P, DEC_BATCH * PAGES], U32)
        nm, sm = a.sb("nm", [P, 3]), a.sb("sm", [P, 3])
        cf = a.sb("cf", [P, 3])
        score, low, drop = a.sb("score", [P, 16]), a.sb("low", [P, 1]), a.sb("drop", [P, 16])
        o = a.sb("o", [P, P])
        o2 = a.sb("o2", [P, P])
        p_s = [a.ps(f"p_s{i}", [P, 512]) for i in range(2)]
        p_w = a.ps("p_w", [P, WIN])
        p_n = a.ps("p_n", [P, 4, 32])
        p_t = [a.ps(f"p_t{i}", [P, 4, P]) for i in range(2)]
        p_o = a.ps("p_o", [P, 3, P])
        table_in, row_ok, idx_ok = a.sem("table_in"), a.sem("row_ok"), a.sem("idx_ok")
        page_in = [a.sem(f"page_in{i}") for i in range(NQB)]
        win_in = [a.sem(f"win_in{i}") for i in range(NQB)]
        a_mm, a_ok, d_mm, d_ok = a.sem("a_mm"), a.sem("a_ok"), a.sem("d_mm"), a.sem("d_ok")
        s_mm, c_mm, c_lg, c_e, lg_ok, pn_ok, imp_mm, nm_ok, e_ok, pv_mm, o_ok = (a.sem(n) for n in (
            "s_mm", "c_mm", "c_lg", "c_e", "lg_ok", "pn_ok", "imp_mm", "nm_ok", "e_ok", "pv_mm", "o_ok"))
        chain = a.sem("chain")
        block = ctx.enter_context(nc.Block())

        def new_v(c):
            return S.h_tok[0:NEW, TILES - 1, c:c + P]

        @block.sync
        def _(sp):
            sp.dma_start(table[:, :], I["page_table"].rearrange("b n -> (b n)").unsqueeze(0)
                         .to_broadcast([P, DEC_BATCH * PAGES])).then_inc(table_in, 16)
            for bb in range(2):
                for b in range(NQB):
                    if bb == 1:
                        sp.wait_ge(win_in[b], 16)
                        sp.wait_ge(pv_mm, b + 1)
                    sp.dma_start(win[:, b, :, :], I["state_win_kv"][0, NQB * bb + b].rearrange(
                        "(k p) s g d -> p k (s g d)", p=P)).then_inc(win_in[b], 16)

        @block.gpsimd
        def _(pool):
            pool.iota(row[:, :], [[0, 1]], base=0, channel_multiplier=1).then_inc(row_ok, 1)
            pool.wait_ge(idx_ok, 1)
            cache = I["cache_nsa_kv"][0].rearrange("n p s g d -> (n p) (s g d)")
            for bb in range(2):
                for b in range(NQB):
                    if bb == 1:
                        pool.wait_ge(page_in[b], 16 * PAGES)
                        pool.wait_ge(pv_mm, b + 1)
                    for n in range(PAGES):
                        c = (NQB * bb + b) * PAGES + n
                        pool.indirect_dma_start(pages[:, b, n, :], None, cache,
                                                bass.IndirectOffsetOnAxis(idx[:, c:c + 1], 0))\
                            .then_inc(page_in[b], 16)

        @block.tensor
        def _(pe):
            def fill(bb, b):
                i = NQB * bb + b
                ua, ud = A_USES * bb + 2 * b, D_USES * bb + 2 * b
                pe.wait_ge(page_in[b], 16 * PAGES * (bb + 1))
                pe.wait_ge(win_in[b], 16 * (bb + 1))
                if ua:
                    pe.wait_ge(a_ok, ua)
                for n in range(4):
                    mm = pe.transpose(p_t[0][:, n, :], pages[:, b, n, 2 * P:3 * P], S.ident[:, :])
                mm.then_inc(a_mm, 1)
                if ud:
                    pe.wait_ge(d_ok, ud)
                for n in range(4):
                    mm = pe.transpose(p_t[1][:, n, :], pages[:, b, 4 + n, 2 * P:3 * P], S.ident[:, :])
                mm.then_inc(d_mm, 1)
                pe.wait_ge(a_ok, ua + 1)
                for n in range(4):
                    mm = pe.transpose(p_t[0][:, n, :], win[:, b, n, 0:P], S.ident[:, :])
                mm.then_inc(a_mm, 1)
                pe.wait_ge(d_ok, ud + 1)
                for n in range(PAGES):
                    pe.matmul(p_t[1][:, 0, 4 * n:4 * n + 4], pages[:, b, n, 0:P], S.mean[:, CB - 4:CB],
                              start=True, stop=True)
                for n in range(PAGES):
                    mm = pe.matmul(p_t[1][0:CB, 1, :], S.mean[:, CB - 4 - 4 * n:2 * CB - 4 - 4 * n],
                                   pages[:, b, n, VC:VC + P], start=(n == 0), stop=(n == PAGES - 1))
                mm.then_inc(d_mm, 1)

            def scores(bb, b):
                i = NQB * bb + b
                q = S.qbd[:, i, :, :, :].rearrange("p g j t -> p (g j t)")
                rows = slice(32 * b, 32 * b + 32)
                pe.wait_ge(a_ok, A_USES * bb + 2 * b + 2)
                pe.wait_ge(d_ok, D_USES * bb + 2 * b + 2)
                for h in range(2):
                    pe.matmul(p_s[h][rows, :], q, kT[:, b % 2, 512 * h:512 * h + 512], start=True, stop=True)
                pe.matmul(p_w[rows, :], q, kwT[:, b % 2, :], start=True, stop=True)
                mm = pe.matmul(p_n[rows, 2, :], q, kc[:, b % 2, :], start=True, stop=True)
                mm.then_inc(s_mm, 1)

            for bb in range(2):
                if bb == 1:
                    pe.wait_ge(nm_ok, 1)
                q4 = S.qbd[:, NQB * bb:NQB * bb + NQB, :, :, :].rearrange("p b g j t -> p (b g j t)")
                for br in range(2):
                    pe.matmul(p_n[:, br, :], q4, S.kT[:, br, SEQ:TOK], start=True, stop=True).then_inc(c_mm, 1)
                for b in range(NQB + 1):
                    if b < NQB:
                        fill(bb, b)
                    if b >= 1:
                        scores(bb, b - 1)
                pe.wait_ge(pn_ok, bb + 1)
                pe.matmul(p_n[:, 3, :], S.peers[:, :], lc[:, :], start=True, stop=True).then_inc(imp_mm, 1)
                ua, ud = A_USES * bb + 2 * NQB, D_USES * bb + 2 * NQB
                pe.wait_ge(e_ok, 2 * bb + 1)
                for n in range(4):
                    mm = pe.transpose(p_t[0][:, n, :], ls[:, n * P:(n + 1) * P], S.ident[:, :])
                mm.then_inc(a_mm, 1)
                for n in range(4):
                    mm = pe.transpose(p_t[1][:, n, :], ls[:, (4 + n) * P:(5 + n) * P], S.ident[:, :])
                mm.then_inc(d_mm, 1)
                pe.wait_ge(e_ok, 2 * bb + 2)
                pe.wait_ge(a_ok, ua + 1)
                for n in range(4):
                    mm = pe.transpose(p_t[0][:, n, :], lw[:, n * P:(n + 1) * P], S.ident[:, :])
                mm.then_inc(a_mm, 1)
                pe.wait_ge(d_ok, ud + 1)
                pe.transpose(p_t[1][0:NEW, 0, :], ls[:, PAST:PAST + NEW], S.ident[:, :])
                pe.transpose(p_t[1][0:NEW, 1, :], lw[:, WIN:WIN + NEW], S.ident[:, :])
                pe.transpose(p_t[1][0:CB, 2, :], lc[:, :], S.ident[:, :]).then_inc(d_mm, 1)
                pe.wait_ge(a_ok, ua + 2)
                pe.wait_ge(d_ok, ud + 2)
                if bb == 1:
                    pe.wait_ge(o_ok, 1)
                for b in range(NQB):
                    rows = slice(32 * b, 32 * b + 32)
                    for n in range(PAGES):
                        pe.matmul(p_o[rows, 1, :], pts[:, n, rows], pages[:, b, n, VS:VS + P],
                                  start=(n == 0), stop=False)
                    pe.matmul(p_o[rows, 1, :], ptn[:, 0, rows], new_v(C_KV + 3 * P), start=False, stop=True)
                    for n in range(4):
                        pe.matmul(p_o[rows, 2, :], ptw[:, n, rows], win[:, b, n, P:2 * P],
                                  start=(n == 0), stop=False)
                    pe.matmul(p_o[rows, 2, :], ptn[:, 1, rows], new_v(C_WIN + P), start=False, stop=True)
                    pe.matmul(p_o[rows, 0, :], ptn[:, 2, rows], vc[:, b, :], start=True, stop=True)\
                        .then_inc(pv_mm, 1)
                pe.wait_ge(o_ok, bb + 1)
                pe.transpose(p_t[0][:, 0, :], o2[:, :], S.ident[:, :]).then_inc(a_mm, 1)

        @block.vector
        def _(dve):
            step = Chain(dve, chain)
            dve.wait_ge(table_in, 16)
            dve.wait_ge(row_ok, 1)
            step(dve.tensor_copy(rowf[:, :], row[:, :]))
            dve.tensor_scalar(idx[:, :], table[:, :], float(P), rowf[:, 0:1], ALU.mult, ALU.add).then_inc(idx_ok, 1)
            step(dve.memset(nb[:, :, :, :], NEG))
            for bb in range(2):
                step(dve.tensor_tensor(nb[:, bb, NQB * bb:NQB * bb + NQB, :],
                                       S.other_seq[:, :].unsqueeze(2).to_broadcast([P, NQB, DEC_SEQ]),
                                       S.bias_s[:, PAST:PAST + DEC_SEQ].unsqueeze(1)
                                       .to_broadcast([P, NQB, DEC_SEQ]), ALU.add))
            for bb in range(2):
                for b in range(NQB):
                    i, ud = NQB * bb + b, D_USES * bb + 2 * b
                    dve.wait_ge(d_mm, ud + 1)
                    if i >= 2:
                        dve.wait_ge(s_mm, i - 1)
                    dve.tensor_copy(kT[:, b % 2, 512:].rearrange("p (n c) -> p n c", c=P), p_t[1][:, :, :])\
                        .then_inc(d_ok, 1)
                    dve.wait_ge(d_mm, ud + 2)
                    if bb == 1:
                        dve.wait_ge(pv_mm, NQB)
                    dve.tensor_copy(vc[:, b, :], p_t[1][0:CB, 1, :])
                    dve.tensor_copy(kc[:, b % 2, :], p_t[1][:, 0, 0:CB]).then_inc(d_ok, 1)
                dve.wait_ge(s_mm, NQB * (bb + 1))
                dve.wait_ge(c_mm, 2 * (bb + 1))
                step(dve.tensor_tensor(lc[:, :], p_n[:, 2, :], S.bias_s[:, 31:PAST:32], ALU.add))
                step(dve.tensor_reduce(nm[:, 0:1], lc[:, :], AX.X, ALU.max))
                dve.tensor_scalar(nm[:, 0:1], nm[:, 0:1], -1.0, None, ALU.mult).then_inc(c_lg, 1)
                new = nb[:, bb, :, :].rearrange("p b t -> p (b t)")
                for h in range(2):
                    c = slice(512 * h, 512 * h + 512)
                    step(dve.tensor_tensor(ls[:, c], p_s[h][:, :], S.bias_s[:, c], ALU.add))
                step(dve.tensor_tensor(ls[:, PAST:PAST + NEW], p_n[:, 0, :], new, ALU.add))
                step(dve.tensor_tensor(lw[:, 0:WIN], p_w[:, :], S.bias_w[:, :], ALU.add))
                step(dve.tensor_tensor(lw[:, WIN:WIN + NEW], p_n[:, 1, :], new, ALU.add))
                dve.wait_ge(c_e, bb + 1)
                step(dve.tensor_scalar(sm[:, 0:1], sm[:, 0:1], 1e-30, None, ALU.max))
                step(dve.reciprocal(cf[:, 0:1], sm[:, 0:1]))
                dve.tensor_scalar(lc[:, :], lc[:, :], cf[:, 0:1], None, ALU.mult).then_inc(pn_ok, 1)
                dve.wait_ge(imp_mm, bb + 1)
                step(dve.tensor_reduce(score[:, :], p_n[:, 3, :].rearrange("p (n two) -> p n two", two=2),
                                       AX.X, ALU.add))
                step(dve.tensor_reduce(low[:, :], score[:, LO:HI], AX.X, ALU.min))
                step(dve.tensor_scalar(drop[:, LO:HI], score[:, LO:HI], low[:, 0:1], None, ALU.is_le))
                step(dve.tensor_tensor(drop[:, LO:HI], drop[:, LO:HI], S.index16[:, LO:HI], ALU.mult))
                step(dve.tensor_reduce(low[:, :], drop[:, LO:HI], AX.X, ALU.max))
                step(dve.tensor_scalar(drop[:, LO:HI], S.index16[:, LO:HI], low[:, 0:1], NEG, ALU.is_equal, ALU.mult))
                sel = ls[:, LO * 64:HI * 64].rearrange("p (n k) -> p n k", k=64)
                step(dve.tensor_tensor(sel, sel, drop[:, LO:HI].unsqueeze(2).to_broadcast([P, HI - LO, 64]), ALU.add))
                step(dve.tensor_reduce(nm[:, 1:2], ls[:, :], AX.X, ALU.max))
                step(dve.tensor_reduce(nm[:, 2:3], lw[:, :], AX.X, ALU.max))
                dve.tensor_scalar(nm[:, 1:3], nm[:, 1:3], -1.0, None, ALU.mult).then_inc(nm_ok, 1)
                ud = D_USES * bb + 2 * NQB
                dve.wait_ge(d_mm, ud + 1)
                dve.tensor_copy(pts[:, 4:, :], p_t[1][:, :, :]).then_inc(d_ok, 1)
                dve.wait_ge(d_mm, ud + 2)
                dve.tensor_copy(ptn[:, :, :], p_t[1][0:NEW, 0:3, :]).then_inc(d_ok, 1)
                step(dve.memset(cf[:, 0:1], 1.0))
                dve.wait_ge(e_ok, 2 * (bb + 1))
                step(dve.tensor_scalar(sm[:, 1:3], sm[:, 1:3], 1e-30, None, ALU.max))
                step(dve.reciprocal(cf[:, 1:3], sm[:, 1:3]))
                step(dve.tensor_tensor(cf[:, :], cf[:, :], S.gates_s[:, bb, :], ALU.mult))
                dve.wait_ge(pv_mm, NQB * (bb + 1))
                step(dve.tensor_scalar(o[:, :], p_o[:, 0, :], cf[:, 0:1], None, ALU.mult))
                for br in (1, 2):
                    step(dve.scalar_tensor_tensor(out=o[:, :], in0=p_o[:, br, :], scalar=cf[:, br:br + 1],
                                                  in1=o[:, :], op0=ALU.mult, op1=ALU.add))
                step(dve.tensor_scalar(o[:, 0:HD], o[:, 0:HD], S.in_group[:, 0:1], None, ALU.mult))
                step(dve.scalar_tensor_tensor(out=o[:, 0:HD], in0=o[:, HD:P], scalar=S.in_group[:, 1:2],
                                              in1=o[:, 0:HD], op0=ALU.mult, op1=ALU.add))
                dve.tensor_copy(o2[:, :].rearrange("p (two d) -> p two d", two=2),
                                o[:, 0:HD].unsqueeze(1).to_broadcast([P, 2, HD])).then_inc(o_ok, 1)

        @block.scalar
        def _(act):
            for bb in range(2):
                for b in range(NQB):
                    i, ua = NQB * bb + b, A_USES * bb + 2 * b
                    act.wait_ge(a_mm, ua + 1)
                    if i >= 2:
                        act.wait_ge(s_mm, i - 1)
                    act.activation(kT[:, b % 2, 0:512].rearrange("p (n c) -> p n c", c=P), p_t[0][:, :, :],
                                   ACT.Copy).then_inc(a_ok, 1)
                    act.wait_ge(a_mm, ua + 2)
                    act.activation(kwT[:, b % 2, :].rearrange("p (n c) -> p n c", c=P), p_t[0][:, :, :],
                                   ACT.Copy).then_inc(a_ok, 1)
                act.wait_ge(c_lg, bb + 1)
                act.activation(lc[:, :], lc[:, :], ACT.Exp, bias=nm[:, 0:1], accum_out=sm[:, 0:1]).then_inc(c_e, 1)
                act.wait_ge(nm_ok, bb + 1)
                act.activation(ls[:, :], ls[:, :], ACT.Exp, bias=nm[:, 1:2], accum_out=sm[:, 1:2]).then_inc(e_ok, 1)
                act.activation(lw[:, :], lw[:, :], ACT.Exp, bias=nm[:, 2:3], accum_out=sm[:, 2:3]).then_inc(e_ok, 1)
                ua = A_USES * bb + 2 * NQB
                act.wait_ge(a_mm, ua + 1)
                act.activation(pts[:, 0:4, :], p_t[0][:, :, :], ACT.Copy).then_inc(a_ok, 1)
                act.wait_ge(a_mm, ua + 2)
                act.activation(ptw[:, :, :], p_t[0][:, :, :], ACT.Copy).then_inc(a_ok, 1)
                act.wait_ge(a_mm, ua + 3)
                c0 = SEQ + NQB * DEC_SEQ * bb
                for par in range(2):
                    rows = slice(par * HD, (par + 1) * HD)
                    src = p_t[0][rows, 0, :].rearrange("p (b j q t) -> p q j b t", b=NQB, j=4, q=2, t=DEC_SEQ)
                    last = act.activation(S.mixT[rows, GH:KD, c0:c0 + NQB * DEC_SEQ].rearrange(
                        "p j (b t) -> p j b t", t=DEC_SEQ), src[:, par], ACT.Copy)
                last.then_inc(a_ok, 1)


PEERS = 8
KEYS = 128
TOPK = 16
PICKS = PEERS * TOPK
GROUP = 16
SPLIT = 3
FAR = -3e38


def residual_stage(nc, I, O, S, scratch):
    with ExitStack() as ctx:
        a = scope(nc, ctx, "rs")
        w_o = a.sb("w_o", [P, KD, D_MODEL])
        gain = a.sb("gain", [P, D_MODEL])
        x = a.sb("x", [P, 2, D_MODEL])
        hres = a.sb("hres", [P, 2, D_MODEL])
        xn = a.sb("xn", [P, 2, D_MODEL])
        rest = a.sb("rest", [P, D_MODEL])
        junk = a.sb("junk", [P, D_MODEL], BF16)
        part = a.sb("part", [P, 2, SPLIT, D_MODEL], BF16)
        sq, ms, rt, rstd = (a.sb(n, [P, TILES]) for n in ("sq", "ms", "rt", "rstd"))
        acc = [a.ps(f"acc{i}", [P, 2, 512]) for i in range(2)]
        tp = [a.ps(f"tp{i}", [P, 4, P]) for i in range(4)]
        x_in = [a.sem(f"x_in{i}") for i in range(2)]
        w_in, gain_in, mm_ok, h_ok, sq_ok, ms_ok, root_ok, rstd_ok, xn_ok = (a.sem(n) for n in (
            "w_in", "gain_in", "mm_ok", "h_ok", "sq_ok", "ms_ok", "root_ok", "rstd_ok", "xn_ok"))
        tp_mm, tp_a, tp_v, hi_ok, r1_ok, mid_ok, lo_ok = (a.sem(n) for n in (
            "tp_mm", "tp_a", "tp_v", "hi_ok", "r1_ok", "mid_ok", "lo_ok"))
        h_out, part_out = [a.sem(f"h_out{i}") for i in range(2)], [a.sem(f"part_out{i}") for i in range(2)]
        block = ctx.enter_context(nc.Block())

        def x_rows(m):
            return I["x_prompt"][0, m * P:(m + 1) * P, :] if m < TILES - 1 else \
                I["x_sample"].rearrange("b t d -> (b t) d")

        @block.sync
        def _(sp):
            w = I["w_o"][0].rearrange("(k p) n -> p k n", p=P)
            for k in range(0, KD, 2):
                sp.dma_start(w_o[:, k:k + 2, :], w[:, k:k + 2, :]).then_inc(w_in, 16)
            for m in range(2):
                sp.dma_start(x[0:ROWS[m], m % 2, :], x_rows(m)).then_inc(x_in[m % 2], 16)
            sp.dma_start(gain[:, :], I["norm2"].to_broadcast([P, D_MODEL])).then_inc(gain_in, 16)
            for m in range(TILES):
                r, g = ROWS[m], ROWS[m] // GROUP
                sp.wait_ge(h_ok, m + 1)
                sp.dma_start(scratch["hres"][m * P:m * P + r, :], hres[0:r, m % 2, :]).then_inc(h_out[m % 2], 16)
                if m + 2 < TILES:
                    sp.dma_start(x[0:ROWS[m + 2], m % 2, :], x_rows(m + 2)).then_inc(x_in[m % 2], 16)
                sp.wait_ge(lo_ok, m + 1)
                for i in range(SPLIT):
                    sp.dma_start(scratch["parts"][m * P // GROUP:m * P // GROUP + g, i],
                                 part[0:r, m % 2, i, :]).then_inc(part_out[m % 2], 16)
            for i in range(2):
                n = (TILES + 1 - i) // 2
                sp.wait_ge(h_out[i], 16 * n)
                sp.wait_ge(part_out[i], 16 * SPLIT * n)

        @block.tensor
        def _(pe):
            pe.wait_ge(w_in, 16 * KD // 2)

            def turn(m):
                r = ROWS[m]
                pe.wait_ge(xn_ok, m + 1)
                for g in range(2):
                    n = 2 * m + g
                    if n >= 4:
                        pe.wait_ge(tp_v if g else tp_a, (n - 4) // 2 + 1)
                    for k in range(4):
                        mm = pe.transpose(tp[n % 4][:, k, 0:r], xn[0:r, m % 2, (4 * g + k) * P:(4 * g + k + 1) * P],
                                          S.ident[0:r, 0:r])
                    mm.then_inc(tp_mm, 1)

            for m in range(TILES):
                r = ROWS[m]
                if m >= 2:
                    pe.wait_ge(h_ok, m - 1)
                for half in range(2):
                    for k in range(KD):
                        mm = pe.matmul(acc[m % 2][0:r, half, :], S.mixT[:, k, m * P:m * P + r],
                                       w_o[:, k, half * 512:half * 512 + 512], start=(k == 0), stop=(k == KD - 1))
                mm.then_inc(mm_ok, 1)
                if m >= 1:
                    turn(m - 1)
            turn(TILES - 1)

        @block.vector
        def _(dve):
            def keep(m):
                n = 2 * m + 1
                dve.wait_ge(tp_mm, n + 1)
                dve.tensor_copy(S.xnT[:, 4:8, m * P:m * P + ROWS[m]], tp[n % 4][:, :, 0:ROWS[m]]).then_inc(tp_v, 1)

            for m in range(TILES):
                r = ROWS[m]
                dve.wait_ge(mm_ok, m + 1)
                dve.wait_ge(x_in[m % 2], 16 * (m // 2 + 1))
                if m >= 2:
                    dve.wait_ge(h_out[m % 2], 16 * (m // 2))
                dve.tensor_tensor(hres[0:r, m % 2, :], acc[m % 2][0:r, :, :].rearrange("p a b -> p (a b)"),
                                  x[0:r, m % 2, :], ALU.add).then_inc(h_ok, 1)
                dve.wait_ge(sq_ok, m + 1)
                dve.tensor_scalar(ms[0:r, m:m + 1], sq[0:r, m:m + 1], 1.0 / D_MODEL, EPS, ALU.mult,
                                  ALU.add).then_inc(ms_ok, 1)
                dve.wait_ge(root_ok, m + 1)
                dve.reciprocal(rstd[0:r, m:m + 1], rt[0:r, m:m + 1]).then_inc(rstd_ok, 1)
                dve.wait_ge(rstd_ok, m + 1)
                if m == 0:
                    dve.wait_ge(gain_in, 16)
                if m >= 2:
                    dve.wait_ge(tp_mm, 2 * (m - 1))
                    dve.wait_ge(r1_ok, m - 1)
                dve.scalar_tensor_tensor(out=xn[0:r, m % 2, :], in0=hres[0:r, m % 2, :], scalar=rstd[0:r, m:m + 1],
                                         in1=gain[0:r, :], op0=ALU.mult, op1=ALU.mult).then_inc(xn_ok, 1)
                if m >= 1:
                    keep(m - 1)
            keep(TILES - 1)

        @block.scalar
        def _(act):
            for m in range(TILES):
                r = ROWS[m]
                act.wait_ge(h_ok, m + 1)
                if m >= 1:
                    act.wait_ge(sq_ok, m)
                act.activation(junk[0:r, :], hres[0:r, m % 2, :], ACT.Square, accum_out=sq[0:r, m:m + 1])\
                    .then_inc(sq_ok, 1)
                act.wait_ge(ms_ok, m + 1)
                act.activation(rt[0:r, m:m + 1], ms[0:r, m:m + 1], ACT.Sqrt).then_inc(root_ok, 1)
                act.wait_ge(xn_ok, m + 1)
                if m >= 2:
                    act.wait_ge(part_out[m % 2], 16 * SPLIT * (m // 2))
                act.activation(part[0:r, m % 2, 0, :], xn[0:r, m % 2, :], ACT.Copy).then_inc(hi_ok, 1)
                act.wait_ge(tp_mm, 2 * m + 1)
                act.activation(S.xnT[:, 0:4, m * P:m * P + r], tp[(2 * m) % 4][:, :, 0:r], ACT.Copy).then_inc(tp_a, 1)
                act.wait_ge(r1_ok, m + 1)
                act.activation(part[0:r, m % 2, 1, :], rest[0:r, :], ACT.Copy).then_inc(mid_ok, 1)

        @block.gpsimd
        def _(pool):
            for m in range(TILES):
                r = ROWS[m]
                pool.wait_ge(hi_ok, m + 1)
                if m >= 1:
                    pool.wait_ge(lo_ok, m)
                pool.tensor_tensor(rest[0:r, :], xn[0:r, m % 2, :], part[0:r, m % 2, 0, :], ALU.subtract)\
                    .then_inc(r1_ok, 1)
                pool.wait_ge(mid_ok, m + 1)
                pool.tensor_tensor(part[0:r, m % 2, 2, :], rest[0:r, :], part[0:r, m % 2, 1, :], ALU.subtract)\
                    .then_inc(lo_ok, 1)


def retrieve_stage(nc, I, O, S):
    with ExitStack() as ctx:
        a = scope(nc, ctx, "rt")
        wq = a.sb("wq", [P, KD, PEERS * P])
        sub = a.sb("sub", [KEYS, PEERS, P])
        keys = a.sb("keys", [P, PEERS, 2, KEYS])
        qT = a.sb("qT", [P, PEERS, TOK])
        sc = a.sb("sc", [P, 2, 2 * PEERS, KEYS])
        val = a.sb("val", [P, 2 * PEERS, TOPK])
        at = a.sb("at", [P, 2 * PEERS, TOPK], U32)
        atf = a.sb("atf", [P, 2 * PEERS, TOPK])
        cand = a.sb("cand", [P, PEERS, TOPK, TOPK])
        top = a.sb("top", [P, PEERS, TOPK])
        pos = a.sb("pos", [P, PEERS, TOPK], U32)
        half = a.sb("half", [P, 2, PEERS, TOPK], U32)
        halff = a.sb("halff", [P, 2, PEERS, TOPK])
        hit = a.sb("hit", [P, PEERS, TOPK, TOPK])
        ids = a.sb("ids", [P, 2, PEERS, TOPK])
        eid = a.sb("eid", [P, PEERS, TOPK])
        gate = a.sb("gate", [P, PEERS, TOPK])
        tot = a.sb("tot", [P, PEERS])
        pq = [a.ps(f"pq{i}", [P, 512]) for i in range(2)]
        pqs = [a.ps(f"pqs{i}", [P, 512]) for i in range(2)]
        psc = [a.ps(f"psc{i}", [P, 4, KEYS]) for i in range(4)]
        wq_in, sub_in, zero_ok, kt_mm, kt_ok, q_mm, qa_ok, qv_ok = (a.sem(n) for n in (
            "wq_in", "sub_in", "zero_ok", "kt_mm", "kt_ok", "q_mm", "qa_ok", "qv_ok"))
        sc_mm, sc_ok, sc_used, top_ok, exp_ok, gate_ok, t_mm, t_ok = (a.sem(n) for n in (
            "sc_mm", "sc_ok", "sc_used", "top_ok", "exp_ok", "gate_ok", "t_mm", "t_ok"))
        chain = a.sem("chain")
        block = ctx.enter_context(nc.Block())

        @block.sync
        def _(sp):
            sp.dma_start(sub[:, :, :].rearrange("n h (c d) -> n h c d", c=2),
                         I["peer_subkeys"][0].rearrange("h c n d -> n h c d")).then_inc(sub_in, 16)
            w = I["peer_wq"][0].rearrange("(k p) n -> p k n", p=P)
            for k in range(0, KD, 2):
                sp.dma_start(wq[:, k:k + 2, :], w[:, k:k + 2, :]).then_inc(wq_in, 16)

        @block.gpsimd
        def _(pool):
            pool.memset(keys[:, :, :, :], 0.0).then_inc(zero_ok, 1)

        @block.tensor
        def _(pe):
            pe.wait_ge(sub_in, 16)
            for n in range(2):
                for h in range(4):
                    mm = pe.transpose(psc[n][:, h, :], sub[:, 4 * n + h, :], S.ident[:, :])
                mm.then_inc(kt_mm, 1)
            pe.wait_ge(wq_in, 16 * KD // 2)
            for h in range(PEERS):
                if h >= 2:
                    pe.wait_ge(qa_ok, h - 1)
                    pe.wait_ge(qv_ok, h - 1)
                for k in range(KD):
                    w = wq[:, k, h * P:(h + 1) * P]
                    pe.matmul(pqs[h % 2][:, 0:NSAMP], w, S.xnT[:, k, SEQ:TOK], start=(k == 0), stop=(k == KD - 1))
                    mm = pe.matmul(pq[h % 2][:, :], w, S.xnT[:, k, 0:SEQ], start=(k == 0), stop=(k == KD - 1))
                mm.then_inc(q_mm, 1)
            pe.wait_ge(kt_ok, 2)
            pe.wait_ge(qa_ok, PEERS)
            pe.wait_ge(qv_ok, PEERS)

            def scores(m):
                r = ROWS[m]
                for n in range(4):
                    if m >= 1:
                        pe.wait_ge(sc_ok, 4 * (m - 1) + n + 1)
                    for j in range(2):
                        h = 2 * n + j
                        mm = pe.matmul(psc[n][0:r, 2 * j:2 * j + 2, :], qT[:, h, m * P:m * P + r],
                                       keys[:, h, :, :], start=True, stop=True)
                    mm.then_inc(sc_mm, 1)

            scores(0)
            for m in range(TILES):
                r = ROWS[m]
                if m + 1 < TILES:
                    scores(m + 1)
                pe.wait_ge(gate_ok, m + 1)
                if m >= 2:
                    pe.wait_ge(t_ok, m - 1)
                pe.transpose(pq[m % 2][:, 0:r], eid[0:r, :, :].rearrange("p h k -> p (h k)"), S.ident[0:r, 0:r])
                pe.transpose(pq[m % 2][:, P:P + r], gate[0:r, :, :].rearrange("p h k -> p (h k)"),
                             S.ident[0:r, 0:r]).then_inc(t_mm, 1)

        @block.vector
        def _(dve):
            step = Chain(dve, chain)
            dve.wait_ge(zero_ok, 1)
            for n in range(2):
                dve.wait_ge(kt_mm, n + 1)
                for c in range(2):
                    rows = slice(c * HD, (c + 1) * HD)
                    last = dve.tensor_copy(keys[rows, 4 * n:4 * n + 4, c, :], psc[n][rows, :, :])
                last.then_inc(kt_ok, 1)
            for h in range(PEERS):
                dve.wait_ge(q_mm, h + 1)
                dve.tensor_copy(qT[:, h, SEQ:TOK], pqs[h % 2][:, 0:NSAMP]).then_inc(qv_ok, 1)

            def best(vals, n, src, where):
                for lo in (0, 8):
                    for i in range(n):
                        last = dve.max(vals(i)[:, lo:lo + 8], src(i))
                    step(last)
                    for i in range(n):
                        last = dve.max_index(where(i)[:, lo:lo + 8], vals(i)[:, lo:lo + 8], src(i))
                    step(last)
                    if lo == 0:
                        for i in range(n):
                            last = dve.match_replace(src(i), vals(i)[:, 0:8], src(i), FAR)
                        step(last)

            for m in range(TILES):
                r = ROWS[m]
                dve.wait_ge(sc_ok, 4 * (m + 1))
                best(lambda i: val[0:r, i, :], 2 * PEERS, lambda i: sc[0:r, m % 2, i, :], lambda i: at[0:r, i, :])
                dve.tensor_copy(atf[0:r, :, :], at[0:r, :, :]).then_inc(sc_used, 1)
                v = val[0:r, :, :].rearrange("p (h c) k -> p h c k", c=2)
                shape = [r, PEERS, TOPK, TOPK]
                step(dve.tensor_tensor(cand[0:r, :, :, :], v[:, :, 0, :].unsqueeze(3).to_broadcast(shape),
                                       v[:, :, 1, :].unsqueeze(2).to_broadcast(shape), ALU.add))
                if m >= 1:
                    dve.wait_ge(exp_ok, m)
                best(lambda h: top[0:r, h, :], PEERS, lambda h: cand[0:r, h, :, :].rearrange("p a b -> p (a b)"),
                     lambda h: pos[0:r, h, :])
                if m >= 1:
                    dve.wait_ge(t_mm, m)
                dve.tensor_tensor(gate[0:r, :, :], top[0:r, :, :], top[0:r, :, 0:1].to_broadcast([r, PEERS, TOPK]),
                                  ALU.subtract).then_inc(top_ok, 1)
                step(dve.tensor_scalar(half[0:r, 0, :, :], pos[0:r, :, :], 4, None, ALU.logical_shift_right))
                step(dve.tensor_scalar(half[0:r, 1, :, :], pos[0:r, :, :], TOPK - 1, None, ALU.bitwise_and))
                step(dve.tensor_copy(halff[0:r, :, :, :], half[0:r, :, :, :]))
                f = atf[0:r, :, :].rearrange("p (h c) k -> p h c k", c=2)
                for c in range(2):
                    step(dve.tensor_tensor(hit[0:r, :, :, :], halff[0:r, c, :, :].unsqueeze(3).to_broadcast(shape),
                                           S.index16[0:r, :].unsqueeze(1).unsqueeze(1).to_broadcast(shape),
                                           ALU.is_equal))
                    step(dve.tensor_tensor(hit[0:r, :, :, :], hit[0:r, :, :, :],
                                           f[:, :, c, :].unsqueeze(2).to_broadcast(shape), ALU.mult))
                    step(dve.tensor_reduce(ids[0:r, c, :, :], hit[0:r, :, :, :], AX.X, ALU.add))
                step(dve.scalar_tensor_tensor(out=eid[0:r, :, :], in0=ids[0:r, 0, :, :], scalar=float(KEYS),
                                              in1=ids[0:r, 1, :, :], op0=ALU.mult, op1=ALU.add))
                dve.wait_ge(exp_ok, m + 1)
                step(dve.tensor_reduce(tot[0:r, :], gate[0:r, :, :], AX.X, ALU.add))
                step(dve.reciprocal(tot[0:r, :], tot[0:r, :]))
                dve.tensor_tensor(gate[0:r, :, :], gate[0:r, :, :], tot[0:r, :].unsqueeze(2)
                                  .to_broadcast([r, PEERS, TOPK]), ALU.mult).then_inc(gate_ok, 1)

        @block.scalar
        def _(act):
            for h in range(PEERS):
                act.wait_ge(q_mm, h + 1)
                act.activation(qT[:, h, 0:SEQ], pq[h % 2][:, :], ACT.Copy).then_inc(qa_ok, 1)

            def keep_scores(m):
                r = ROWS[m]
                for n in range(4):
                    act.wait_ge(sc_mm, 4 * m + n + 1)
                    if m >= 2:
                        act.wait_ge(sc_used, m - 1)
                    act.activation(sc[0:r, m % 2, 4 * n:4 * n + 4, :], psc[n][0:r, :, :], ACT.Copy).then_inc(sc_ok, 1)

            keep_scores(0)
            for m in range(TILES):
                r = ROWS[m]
                if m + 1 < TILES:
                    keep_scores(m + 1)
                act.wait_ge(top_ok, m + 1)
                act.activation(gate[0:r, :, :], gate[0:r, :, :], ACT.Exp).then_inc(exp_ok, 1)
                act.wait_ge(t_mm, m + 1)
                act.activation(S.pick[:, m * P:m * P + r], pq[m % 2][:, 0:r], ACT.Copy)
                act.activation(S.gate[:, m * P:m * P + r], pq[m % 2][:, P:P + r], ACT.Copy).then_inc(t_ok, 1)


def experts_stage(nc, I, O, S, scratch):
    G = TOK // GROUP
    QUADS, Q = GROUP // 4, 4
    LAG = 5
    AHEAD = 2
    with ExitStack() as ctx:
        a = scope(nc, ctx, "ex")
        u = a.sb("u", [P, GROUP, D_MODEL])
        v = a.sb("v", [P, GROUP, D_MODEL])
        idx = a.sb("idx", [P, 2, GROUP], U32)
        rows = a.sb("rows", [SPLIT * GROUP, 2, D_MODEL], BF16)
        sel = a.sb("sel", [SPLIT * GROUP, GROUP, P], BF16)
        rowi, rowf = a.sb("rowi", [P, 1], I32), a.sb("rowf", [P, 1])
        prod = a.sb("prod", [P, 2, D_MODEL])
        dots, ge = a.sb("dots", [P, GROUP]), a.sb("ge", [P, GROUP])
        w = a.sb("w", [P, GROUP * GROUP])
        hr = a.sb("hr", [GROUP, 2, D_MODEL])
        y = a.sb("y", [GROUP, 2, D_MODEL])
        xb = [a.ps(f"xb{i}", [P, 2, 512]) for i in range(2)]
        out = [a.ps(f"out{i}", [GROUP, 2, 512]) for i in range(2)]
        u_in, v_in = [a.sem(f"u_in{i}") for i in range(QUADS)], [a.sem(f"v_in{i}") for i in range(QUADS)]
        rows_in, hr_in, y_out = ([a.sem(f"{n}{i}") for i in range(2)] for n in ("rows_in", "hr_in", "y_out"))
        row_ok, sel_ok, w_zero, idx_ok, xb_mm, dot_ok, ge_ok, w_ok, v_used, out_mm, y_ok = (a.sem(n) for n in (
            "row_ok", "sel_ok", "w_zero", "idx_ok", "xb_mm", "dot_ok", "ge_ok", "w_ok", "v_used", "out_mm", "y_ok"))
        chain, turns = a.sem("chain"), a.sem("turns")
        block = ctx.enter_context(nc.Block())

        def over_groups(eng, group):
            group(0, 0, True, False)
            with eng.Fori(0, (G - 2) // 2, 1) as i:
                group(i * 2 + 1, 1, False, False)
                group(i * 2 + 2, 0, False, False)
            group(G - 1, (G - 1) % 2, False, True)

        def ds(start, n):
            return slice(start, start + n) if isinstance(start, int) else bass.ds(start, n)

        def transfers(g, par):
            return (g + 2 - par) * 8

        @block.sync
        def _(sp):
            def load_rows(g, par):
                sp.dma_start(rows[:, par, :], scratch["parts"].rearrange("g i t d -> (g i t) d")
                             [ds(g * (SPLIT * GROUP), SPLIT * GROUP), :]).then_inc(rows_in[par], 16)

            def load_residual(g, par):
                sp.dma_start(hr[:, par, :], scratch["hres"][ds(g * GROUP, GROUP), :]).then_inc(hr_in[par], 16)

            def store(g, par, sample):
                dst = I_rows["sample"][g * GROUP - SEQ:g * GROUP - SEQ + GROUP, :] if sample else \
                    I_rows["prompt"][ds(g * GROUP, GROUP), :]
                sp.dma_start(dst, y[:, par, :]).then_inc(y_out[par], 16)

            I_rows = dict(prompt=O["y_prompt"][0], sample=O["y_sample"].rearrange("b t d -> (b t) d"))

            def group(g, par, first, last):
                if first:
                    for n in range(2):
                        load_rows(n, n)
                        load_residual(n, n)
                    return
                if not last:
                    sp.wait_ge(xb_mm, g * GROUP)
                    load_rows(g + 1, 1 - par)
                sp.wait_ge(y_ok, g + 1)
                if not last:
                    load_residual(g + 1, 1 - par)
                store(g - 1, 1 - par, last)

            for i in range(2):
                sp.sem_inc(y_out[i], 16)
            over_groups(sp, group)
            sp.wait_ge(y_ok, G + 1)
            store(G - 1, (G - 1) % 2, True)
            for i in range(2):
                sp.wait_ge(y_out[i], 16 * (G // 2 + 1))

        @block.gpsimd
        def _(pool):
            pool.iota(rowi[:, :], [[0, 1]], base=0, channel_multiplier=1).then_inc(row_ok, 1)
            pool.memset(w[:, :], 0.0).then_inc(w_zero, 1)

            def gather(table, slots, arrived, par, q):
                pool.sem_inc(turns, 1)
                for t in range(Q * q, Q * q + Q):
                    pool.indirect_dma_start(slots[:, t, :], None, table,
                                            bass.IndirectOffsetOnAxis(idx[:, par, t:t + 1], 0))\
                        .then_inc(arrived[q], 16)

            pool.wait_ge(idx_ok, 2)
            for q in range(QUADS):
                gather(I["peer_u"][0], u, u_in, 0, q)
                gather(I["peer_v"][0], v, v_in, 0, q)

            def group(g, par, first, last):
                if last:
                    return
                pool.wait_ge(idx_ok, g + 2)
                for q in range(QUADS):
                    pool.wait_ge(dot_ok, g * GROUP + Q * q + Q)
                    gather(I["peer_u"][0], u, u_in, 1 - par, q)
                    pool.wait_ge(v_used, g * QUADS + q + 1)
                    gather(I["peer_v"][0], v, v_in, 1 - par, q)

            over_groups(pool, group)

        @block.tensor
        def _(pe):
            def broadcast(par, t):
                for half in range(2):
                    mm = pe.matmul(xb[t % 2][:, half, :], sel[:, t, :], rows[:, par, half * 512:half * 512 + 512],
                                   start=True, stop=True)
                mm.then_inc(xb_mm, 1)

            def combine(g, par, t):
                q = t // Q
                if t % Q == 0:
                    pe.wait_ge(w_ok, g * QUADS + q + 1)
                    pe.wait_ge(v_in[q], (g + 1) * (16 * Q))
                for half in range(2):
                    mm = pe.matmul(out[par][:, half, :], w[:, t * GROUP:(t + 1) * GROUP],
                                   v[:, t, half * 512:half * 512 + 512], start=(t == 0), stop=(t == GROUP - 1))
                if t % Q == Q - 1:
                    mm.then_inc(v_used, 1)

            pe.wait_ge(sel_ok, 1)
            pe.wait_ge(rows_in[0], 16)
            for t in range(AHEAD):
                broadcast(0, t)

            def group(g, par, first, last):
                for t in range(GROUP):
                    pe.wait_ge(dot_ok, g * GROUP + t + 1)
                    if t + AHEAD < GROUP:
                        broadcast(par, t + AHEAD)
                    elif not last:
                        if t + AHEAD == GROUP:
                            pe.wait_ge(rows_in[1 - par], transfers(g + 1, 1 - par))
                        broadcast(1 - par, t + AHEAD - GROUP)
                    if t >= LAG:
                        combine(g, par, t - LAG)
                    elif not first:
                        combine(g - 1, 1 - par, t - LAG + GROUP)
                if last:
                    for t in range(GROUP - LAG, GROUP):
                        combine(g, par, t)

            over_groups(pe, group)

        @block.vector
        def _(dve):
            step = Chain(dve, chain)
            dve.wait_ge(row_ok, 1)
            step(dve.tensor_scalar(rowi[:, :], rowi[:, :], GROUP - 1, None, ALU.bitwise_and))
            step(dve.tensor_copy(rowf[:, :], rowi[:, :]))
            n = SPLIT * GROUP
            dve.tensor_scalar(sel[:, :, :], S.index16[0:n, :].unsqueeze(2).to_broadcast([n, GROUP, P]),
                              rowf[0:n, 0:1], None, ALU.is_equal).then_inc(sel_ok, 1)
            dve.wait_ge(w_zero, 1)
            dve.sem_inc(y_ok, 1)

            def weights(g, q):
                dve.wait_ge(ge_ok, g * QUADS + q + 1)
                if not isinstance(g, int) or g > 0:
                    dve.wait_ge(v_used, g * QUADS + q - (QUADS - 1))
                at = (GROUP + 1) * Q * q
                dve.tensor_tensor(w[:, at:at + (GROUP + 1) * (Q - 1) + 1:GROUP + 1], ge[:, Q * q:Q * q + Q],
                                  S.gate[:, ds(g * GROUP + Q * q, Q)], ALU.mult).then_inc(w_ok, 1)

            def finish(g, par):
                dve.wait_ge(v_used, g * QUADS + QUADS)
                dve.wait_ge(hr_in[par], transfers(g, par))
                dve.wait_ge(y_out[par], transfers(g, par))
                dve.tensor_tensor(y[:, par, :], out[par][:, :, :].rearrange("p a b -> p (a b)"), hr[:, par, :],
                                  ALU.add).then_inc(y_ok, 1)

            def group(g, par, first, last):
                for t in range(GROUP):
                    if t % Q == 0:
                        dve.wait_ge(u_in[t // Q], (g + 1) * (16 * Q))
                    dve.wait_ge(xb_mm, g * GROUP + t + 1)
                    if not first or t >= 2:
                        dve.wait_ge(dot_ok, g * GROUP + t - 1)
                    dve.tensor_tensor_reduce(prod[:, t % 2, :], u[:, t, :],
                                             xb[t % 2][:, :, :].rearrange("p a b -> p (a b)"), 1.0, 0.0,
                                             ALU.mult, ALU.add, dots[:, t:t + 1]).then_inc(dot_ok, 1)
                    if t % Q == 0:
                        if t > 0:
                            weights(g, t // Q - 1)
                        elif not first:
                            weights(g - 1, QUADS - 1)
                    if t == 2 * Q and not first:
                        finish(g - 1, 1 - par)
                if last:
                    weights(g, QUADS - 1)
                    finish(g, par)

            over_groups(dve, group)

        @block.scalar
        def _(act):
            for n in range(2):
                act.activation(idx[:, n, :], S.pick[:, n * GROUP:(n + 1) * GROUP], ACT.Copy).then_inc(idx_ok, 1)

            def group(g, par, first, last):
                if not first and not last:
                    for q in range(QUADS):
                        act.wait_ge(u_in[q], g * (16 * Q))
                        act.wait_ge(v_in[q], g * (16 * Q))
                    act.activation(idx[:, 1 - par, :], S.pick[:, ds((g + 1) * GROUP, GROUP)], ACT.Copy)\
                        .then_inc(idx_ok, 1)
                for q in range(QUADS):
                    act.wait_ge(dot_ok, g * GROUP + Q * q + Q)
                    if not first:
                        act.wait_ge(w_ok, g * QUADS + q - (QUADS - 1))
                    act.activation(ge[:, Q * q:Q * q + Q], dots[:, Q * q:Q * q + Q], ACT.Gelu).then_inc(ge_ok, 1)

            over_groups(act, group)


def shared_constants(nc, ctx, S):
    a = scope(nc, ctx, "sc")
    S.ident = a.sb("ident", [P, P])
    S.index16 = a.sb("index16", [P, TOPK])


def shared_route(nc, ctx, S):
    a = scope(nc, ctx, "sr")
    S.pick = a.sb("pick", [P, TOK], U32)
    S.gate = a.sb("gate", [P, TOK])


def shared_rows(nc, ctx, S):
    S.xnT = scope(nc, ctx, "sx").sb("xnT", [P, KD, TOK])


def shared(nc, ctx, S):
    a = scope(nc, ctx, "sh")
    S.ones, S.upper, S.neg_strict, S.neg_upper = (
        a.sb(n, [P, P]) for n in "ones upper neg_strict neg_upper".split())
    S.join = a.sb("join", [P, LEVELS, P])
    S.seq_ones, S.seq_upper, S.seq_neg_strict, S.seq_neg_upper = (
        a.sb(n, [NSAMP, NSAMP]) for n in "seq_ones seq_upper seq_neg_strict seq_neg_upper".split())
    S.seq_pick = a.sb("seq_pick", [NSAMP, DEC_BATCH])
    S.mean = a.sb("mean", [P, 2 * CB - 4])
    S.mean_rep = a.sb("mean_rep", [P, TILES - 1, P])
    S.head_rows = a.sb("head_rows", [P, 8])
    S.other_seq = a.sb("other_seq", [P, 4])
    S.peers = a.sb("peers", [P, P])
    S.in_group = a.sb("in_group", [P, 2])
    S.h_tok = a.sb("h_tok", [P, TILES, COLS])
    S.conv_in = a.sb("conv_in", [P, CT, CW])


def shared_delta(nc, ctx, S):
    a = scope(nc, ctx, "sg")
    S.cs = a.sb("cs", [P, CT, TOK])
    S.zs = a.sb("zs", [P, TILES, 512])
    S.nrm = a.sb("nrm", [P, TILES, 8])


def shared_attend(nc, ctx, S):
    a = scope(nc, ctx, "sa")
    S.qT = a.sb("qT", [P, PH, TOK])
    S.kT = a.sb("kT", [P, 2, TOK])
    S.kcT = a.sb("kcT", [P, GROUPS, NB])
    S.vbd = a.sb("vbd", [P, NH, HD])
    S.qbd = a.sb("qbd", [P, DEC_BATCH, GROUPS, PH, DEC_SEQ])
    S.gates = a.sb("gates", [P, TILES, 24])
    S.gates_s = a.sb("gates_s", [P, 2, 3])
    S.bias = a.sb("bias", [P, NH, SEQ])
    S.bias_s = a.sb("bias_s", [P, PAST + DEC_SEQ])
    S.bias_w = a.sb("bias_w", [P, WIN])


def scratch_tensors(nc):
    return {n: nc.dram_tensor(f"scratch_{n}", s, d, kind="Internal").ap() for n, s, d in (
        ("tab", [4, NH, TABLE], F32), ("tabw", [4, NH, WTABLE], F32), ("gates", [DEC_SEQ, DEC_BATCH, 24], F32),
        ("hres", [TOK, D_MODEL], F32), ("parts", [TOK // GROUP, SPLIT, GROUP, D_MODEL], BF16))}


def mix(nc, ctx, S):
    S.mixT = scope(nc, ctx, "mx").sb("mixT", [P, KD, TOK])


def decoder_step(nc, x_prompt, x_sample, cache_nsa_kv, page_table, state_win_kv, state_conv, state_gdn,
                 norm1, w_in, gdn_conv_w, gdn_a_log, gdn_dt_bias, gdn_norm, nsa_q_norm, nsa_k_norm,
                 rel_bias, w_o, norm2, peer_wq, peer_subkeys, peer_u, peer_v,
                 y_prompt, y_sample, kv_rows_prompt, win_prompt, conv_prompt, gdn_prompt,
                 kv_rows_sample, win_sample, conv_sample, gdn_sample):
    I = dict(x_prompt=x_prompt, x_sample=x_sample, cache_nsa_kv=cache_nsa_kv, page_table=page_table,
             state_win_kv=state_win_kv, state_conv=state_conv, state_gdn=state_gdn, norm1=norm1, w_in=w_in,
             gdn_conv_w=gdn_conv_w, gdn_a_log=gdn_a_log, gdn_dt_bias=gdn_dt_bias, gdn_norm=gdn_norm,
             nsa_q_norm=nsa_q_norm, nsa_k_norm=nsa_k_norm, rel_bias=rel_bias, w_o=w_o, norm2=norm2,
             peer_wq=peer_wq, peer_subkeys=peer_subkeys, peer_u=peer_u, peer_v=peer_v)
    O = dict(y_prompt=y_prompt, y_sample=y_sample, kv_rows_prompt=kv_rows_prompt, win_prompt=win_prompt,
             conv_prompt=conv_prompt, gdn_prompt=gdn_prompt, kv_rows_sample=kv_rows_sample,
             win_sample=win_sample, conv_sample=conv_sample, gdn_sample=gdn_sample)
    S = Shared()
    scratch = scratch_tensors(nc)
    with ExitStack() as whole:
        shared_constants(nc, whole, S)
        shared_route(nc, whole, S)
        with ExitStack() as mixing:
            mix(nc, mixing, S)
            with ExitStack() as heads:
                shared(nc, heads, S)
                masks_stage(nc, I, O, S)
                project_stage(nc, I, O, S)
                with ExitStack() as delta:
                    shared_delta(nc, delta, S)
                    conv_stage(nc, I, O, S)
                    delta_stage(nc, I, O, S)
                with ExitStack() as attend:
                    shared_attend(nc, attend, S)
                    keys_stage(nc, I, O, S, scratch)
                    attend_prompt_stage(nc, I, O, S)
                    attend_sample_stage(nc, I, O, S)
            shared_rows(nc, mixing, S)
            residual_stage(nc, I, O, S, scratch)
            retrieve_stage(nc, I, O, S)
        experts_stage(nc, I, O, S, scratch)


_INS = ['x_prompt', 'x_sample', 'cache_nsa_kv', 'page_table', 'state_win_kv', 'state_conv', 'state_gdn',
        'norm1', 'w_in', 'gdn_conv_w', 'gdn_a_log', 'gdn_dt_bias', 'gdn_norm', 'nsa_q_norm', 'nsa_k_norm',
        'rel_bias', 'w_o', 'norm2', 'peer_wq', 'peer_subkeys', 'peer_u', 'peer_v']
_OUTS = [((1, SEQ, D_MODEL), 'float32'), ((DEC_BATCH, DEC_SEQ, D_MODEL), 'float32'),
         ((1, 1, SEQ, 4, GROUPS, HD), 'float32'), ((1, 1, WIN, 2, GROUPS, HD), 'float32'),
         ((1, 1, TAPS - 1, CONV_CH), 'float32'), ((1, 1, GH, P, P), 'float32'),
         ((1, DEC_BATCH, DEC_SEQ, 4, GROUPS, HD), 'float32'), ((1, DEC_BATCH, WIN, 2, GROUPS, HD), 'float32'),
         ((1, DEC_BATCH, TAPS - 1, CONV_CH), 'float32'), ((1, DEC_BATCH, GH, P, P), 'float32')]


def kernel(**inputs):
    import numpy as _np
    import concourse.bacc as _bacc
    from concourse import mybir as _mybir
    from concourse.bass_utils import run_bass_kernel_spmd as _run

    nc = _bacc.Bacc("TRN2", target_bir_lowering=False, num_devices=1)
    arrays, args = {}, []
    for name in _INS:
        a = _np.ascontiguousarray(inputs[name])
        arrays[f"in_{name}_dram"] = a
        args.append(nc.dram_tensor(f"in_{name}_dram", a.shape, _mybir.dt.from_np(a.dtype), kind="ExternalInput").ap())
    for i, (shape, dtype) in enumerate(_OUTS):
        dt = _mybir.dt.from_np(_np.dtype(dtype))
        args.append(nc.dram_tensor(f"out_{i}_dram", shape, dt, kind="ExternalOutput").ap())
    decoder_step(nc, *args)
    r = _run(nc, [arrays], core_ids=[0])
    return tuple(r.results[0][f"out_{i}_dram"] for i in range(len(_OUTS)))
```
